# Optimizing a Trainium2 kernel written in Bass

```python
import math
import jax, jax.numpy as jnp
from jax import lax
import numpy as np

D_MODEL = 1024
BATCH = 1
SEQ = 512
DEPTH = 2

CHUNK = 64
Q_BLOCK = 128
D_RNN = 1024
N_RNN_BLOCKS = 8
RNN_BLOCK = D_RNN // N_RNN_BLOCKS
CONV_WIDTH = 4
LRU_C = 8.0
N_HEADS = 16
HEAD_DIM = 64
D_ATTN = N_HEADS * HEAD_DIM
D_FF = 2816
EPS = 1e-6
N_BRANCH = 2
OFF_LRU_X = 0
OFF_LRU_G = OFF_LRU_X + D_RNN
OFF_Q = OFF_LRU_G + D_RNN
OFF_K = OFF_Q + D_ATTN
OFF_V = OFF_K + D_ATTN
OFF_F = OFF_V + D_ATTN
OFF_GATE = OFF_F + N_HEADS
D_IN = OFF_GATE + N_BRANCH * D_MODEL


def rms_norm(x, g):
    xf = x.astype(jnp.float32)
    y = xf * lax.rsqrt(jnp.mean(xf * xf, axis=-1, keepdims=True) + EPS)
    return (y * g.astype(jnp.float32)).astype(x.dtype)

def swiglu_ffn(h, w_up, w_down):
    gate, up = jnp.split(h @ w_up, 2, axis=-1)
    return (jax.nn.silu(gate) * up) @ w_down

def causal_depthwise_conv(x, w, b):
    y = lax.conv_general_dilated(
        x, w[:, None, :].astype(x.dtype), window_strides=(1,),
        padding=[(CONV_WIDTH - 1, 0)],
        dimension_numbers=("NWC", "WIO", "NWC"),
        feature_group_count=x.shape[-1])
    return y + b

def rg_lru(x, w_a, b_a, w_x, b_x, lam):
    bsz, seq, _ = x.shape
    xb = x.reshape(bsz, seq, N_RNN_BLOCKS, RNN_BLOCK)
    r = jax.nn.sigmoid((jnp.einsum("bsnc,ncd->bsnd", xb, w_a).reshape(bsz, seq, D_RNN) + b_a).astype(jnp.float32))
    i = jax.nn.sigmoid((jnp.einsum("bsnc,ncd->bsnd", xb, w_x).reshape(bsz, seq, D_RNN) + b_x).astype(jnp.float32))
    log_a = -LRU_C * r * jax.nn.softplus(-lam.astype(jnp.float32))
    a = jnp.exp(log_a)
    u = jnp.sqrt(-jnp.expm1(2.0 * log_a)) * (i * x.astype(jnp.float32))

    def combine(left, right):
        a_l, b_l = left
        a_r, b_r = right
        return a_l * a_r, a_r * b_l + b_r

    _, h = lax.associative_scan(combine, (a, u), axis=1)
    return h.astype(x.dtype)

def forgetting_attention(q, k, v, f_logit, g_q, g_k):
    bsz, seq = q.shape[0], q.shape[1]
    qn = rms_norm(q, g_q).transpose(0, 2, 1, 3)
    kn = rms_norm(k, g_k).transpose(0, 2, 1, 3)
    vh = v.transpose(0, 2, 1, 3)
    cum = jnp.cumsum(jax.nn.log_sigmoid(f_logit.astype(jnp.float32)), axis=1).transpose(0, 2, 1)
    scale = HEAD_DIM ** -0.5
    outs = []
    for blk in range(seq // Q_BLOCK):
        q0 = blk * Q_BLOCK
        q1 = q0 + Q_BLOCK
        s = jnp.einsum("bhqd,bhkd->bhqk", qn[:, :, q0:q1], kn[:, :, :q1]).astype(jnp.float32) * scale
        s = s + cum[:, :, q0:q1, None] - cum[:, :, None, :q1]
        mask = jnp.arange(q0, q1)[:, None] >= jnp.arange(q1)[None, :]
        s = jnp.where(mask, s, -jnp.inf)
        p = jax.nn.softmax(s, axis=-1)
        outs.append(jnp.einsum("bhqk,bhkd->bhqd", p.astype(vh.dtype), vh[:, :, :q1]))
    o = jnp.concatenate(outs, axis=2)
    return o.transpose(0, 2, 1, 3).reshape(bsz, seq, D_ATTN)

def first_inputs(seed: int = 0) -> dict:
    key = jax.random.key(seed)
    ks = jax.random.split(key, 24)
    L, D, F = DEPTH, D_MODEL, D_FF
    nrm = lambda k, shape, fan_in: jax.random.normal(k, shape, jnp.float32) * (fan_in ** -0.5)
    gain = lambda k, shape: 1.0 + 0.02 * jax.random.normal(k, shape, jnp.float32)
    small = lambda k, shape: 0.01 * jax.random.normal(k, shape, jnp.float32)
    u = jax.random.uniform(ks[13], (L, D_RNN), jnp.float32, 0.9, 0.999)
    a0 = u ** (1.0 / LRU_C)
    lam = jnp.log(a0) - jnp.log1p(-a0)
    return {
        "x": jax.random.normal(ks[0], (BATCH, SEQ, D), jnp.float32),
        "g_ffn1": gain(ks[1], (L, D)),
        "w_up1": nrm(ks[2], (L, D, 2 * F), D),
        "w_down1": nrm(ks[3], (L, F, D), F),
        "g_mix": gain(ks[4], (L, D)),
        "w_in": nrm(ks[5], (L, D, D_IN), D),
        "b_gate": small(ks[6], (L, N_BRANCH * D)),
        "conv_w": nrm(ks[7], (L, CONV_WIDTH, D_RNN), CONV_WIDTH),
        "conv_b": small(ks[8], (L, D_RNN)),
        "w_a": nrm(ks[9], (L, N_RNN_BLOCKS, RNN_BLOCK, RNN_BLOCK), RNN_BLOCK),
        "b_a": small(ks[10], (L, D_RNN)),
        "w_x": nrm(ks[11], (L, N_RNN_BLOCKS, RNN_BLOCK, RNN_BLOCK), RNN_BLOCK),
        "b_x": small(ks[12], (L, D_RNN)),
        "lam": lam,
        "g_q": gain(ks[14], (L, HEAD_DIM)),
        "g_k": gain(ks[15], (L, HEAD_DIM)),
        "b_forget": jax.random.uniform(ks[16], (L, N_HEADS), jnp.float32, 1.0, 6.0),
        "w_lru_out": nrm(ks[17], (L, D_RNN, D), D_RNN),
        "w_attn_out": nrm(ks[18], (L, D_ATTN, D), D_ATTN),
        "w_o": nrm(ks[19], (L, D, D), D),
        "g_ffn2": gain(ks[20], (L, D)),
        "w_up2": nrm(ks[21], (L, D, 2 * F), D),
        "w_down2": nrm(ks[22], (L, F, D), F),
    }

def first_block(x, g_ffn1, w_up1, w_down1, g_mix, w_in, b_gate, conv_w, conv_b,
              w_a, b_a, w_x, b_x, lam, g_q, g_k, b_forget, w_lru_out, w_attn_out,
              w_o, g_ffn2, w_up2, w_down2):
    bsz, seq, _ = x.shape
    assert seq % CHUNK == 0 and seq % Q_BLOCK == 0
    for l in range(DEPTH):
        x = x + 0.5 * swiglu_ffn(rms_norm(x, g_ffn1[l]), w_up1[l], w_down1[l])

        h = rms_norm(x, g_mix[l])
        z = h @ w_in[l]
        z_lx = z[..., OFF_LRU_X:OFF_LRU_G]
        z_lg = z[..., OFF_LRU_G:OFF_Q]
        q = z[..., OFF_Q:OFF_K].reshape(bsz, seq, N_HEADS, HEAD_DIM)
        k = z[..., OFF_K:OFF_V].reshape(bsz, seq, N_HEADS, HEAD_DIM)
        v = z[..., OFF_V:OFF_F].reshape(bsz, seq, N_HEADS, HEAD_DIM)
        f_logit = z[..., OFF_F:OFF_GATE] + b_forget[l]
        gates = jax.nn.sigmoid(z[..., OFF_GATE:] + b_gate[l])
        gate_lru, gate_attn = jnp.split(gates, N_BRANCH, axis=-1)

        xr = causal_depthwise_conv(z_lx, conv_w[l], conv_b[l])
        hr = rg_lru(xr, w_a[l], b_a[l], w_x[l], b_x[l], lam[l])
        y_lru = (jax.nn.gelu(z_lg) * hr) @ w_lru_out[l]

        o = forgetting_attention(q, k, v, f_logit, g_q[l], g_k[l])
        y_attn = o @ w_attn_out[l]

        m = gate_lru * y_lru + gate_attn * y_attn
        x = x + m @ w_o[l]

        x = x + 0.5 * swiglu_ffn(rms_norm(x, g_ffn2[l]), w_up2[l], w_down2[l])
    return x


DEPTH_2 = 1

MEM_LEN = 256
NEG_INF = -1e30
CONV_WIDTH_2 = 512
CONV_KERNEL = 31
NSA_HEADS = 8
NSA_WIDTH = NSA_HEADS * HEAD_DIM
NSA_KV_GROUPS = 2
HEADS_PER_GROUP = NSA_HEADS // NSA_KV_GROUPS
KV_WIDTH = NSA_KV_GROUPS * HEAD_DIM
MIX_WIDTH = CONV_WIDTH_2 + NSA_WIDTH
ROT_DIM = HEAD_DIM // 4
ROPE_THETA = 500000.0
CMP_BLOCK = 32
CMP_STRIDE = 16
CMP_HIDDEN = 128
SEL_BLOCK = 64
N_SELECT = 16
N_LOCAL_SEL = 2
FORCED_SCORE = 1e9
WINDOW = 512
WIN_Q_BLOCK = 128
SEL_Q_CHUNK = 32
MEM_HEADS = 4
MEM_HEAD_DIM = D_MODEL // MEM_HEADS
PEER_HEADS = 8
PEER_KEYS = 128
PEER_EXPERTS = PEER_KEYS * PEER_KEYS
PEER_QDIM = 256
PEER_HALF = PEER_QDIM // 2
PEER_TOPK = 16
PEER_TOKEN_CHUNK = 128
IN_SIZES = [CONV_WIDTH_2, CONV_WIDTH_2, NSA_WIDTH,
            KV_WIDTH, KV_WIDTH, KV_WIDTH, KV_WIDTH, KV_WIDTH, KV_WIDTH,
            3 * NSA_HEADS]
IN_COLS = sum(IN_SIZES)
IN_SPLITS = [sum(IN_SIZES[:i + 1]) for i in range(len(IN_SIZES) - 1)]


def rmsnorm(x, g):
    xf = x.astype(jnp.float32)
    y = xf * lax.rsqrt(jnp.mean(xf * xf, axis=-1, keepdims=True) + EPS)
    return (y * g.astype(jnp.float32)).astype(x.dtype)

def layernorm(x, g, b):
    xf = x.astype(jnp.float32)
    mu = jnp.mean(xf, axis=-1, keepdims=True)
    var = jnp.mean(jnp.square(xf - mu), axis=-1, keepdims=True)
    y = (xf - mu) * lax.rsqrt(var + EPS) * g.astype(jnp.float32) + b.astype(jnp.float32)
    return y.astype(x.dtype)

def masked_softmax(s, mask):
    s = jnp.where(mask, s.astype(jnp.float32), NEG_INF)
    return jax.nn.softmax(s, axis=-1) * mask

def partial_rope(x, positions):
    half = ROT_DIM // 2
    inv = ROPE_THETA ** (-(jnp.arange(half, dtype=jnp.float32) * 2.0 / ROT_DIM))
    ang = positions.astype(jnp.float32)[..., None] * inv
    cos = jnp.cos(ang)[:, :, None, :]
    sin = jnp.sin(ang)[:, :, None, :]
    xr = x[..., :ROT_DIM].astype(jnp.float32)
    x1, x2 = xr[..., :half], xr[..., half:]
    rot = jnp.concatenate([x1 * cos - x2 * sin, x2 * cos + x1 * sin], axis=-1).astype(x.dtype)
    return jnp.concatenate([rot, x[..., ROT_DIM:]], axis=-1)

def conformer_conv(a, b, w_dw, b_dw, ln_g, ln_b):
    u = a * jax.nn.sigmoid(b)
    y = lax.conv_general_dilated(
        u, w_dw[:, None, :], window_strides=(1,), padding=[(CONV_KERNEL - 1, 0)],
        dimension_numbers=('NWC', 'WIO', 'NWC'), feature_group_count=CONV_WIDTH_2)
    y = layernorm(y + b_dw, ln_g, ln_b)
    return jax.nn.silu(y)

def compress_tokens(kv, pos_emb, w1, b1, w2, b2):
    B, T, G, dh = kv.shape
    n_cmp = (T - CMP_BLOCK) // CMP_STRIDE + 1
    idx = jnp.arange(n_cmp)[:, None] * CMP_STRIDE + jnp.arange(CMP_BLOCK)[None, :]
    blk = kv[:, idx] + pos_emb[:, None, :]
    blk = blk.transpose(0, 1, 3, 2, 4).reshape(B, n_cmp, G, CMP_BLOCK * dh)
    hdn = jax.nn.gelu(blk @ w1 + b1)
    return hdn @ w2 + b2

def nsa_mixer(q, k_c, v_c, k_s, v_s, k_w, v_w, gate_logits, positions,
              cmp_pos, cmp_w1, cmp_b1, cmp_w2, cmp_b2):
    B, T = q.shape[:2]
    G, Hg, dh = NSA_KV_GROUPS, HEADS_PER_GROUP, HEAD_DIM
    scale = dh ** -0.5
    t_idx = jnp.arange(T)
    kvr = lambda t: t.reshape(B, T, G, dh)
    k_c, v_c, k_s, v_s, k_w, v_w = map(kvr, (k_c, v_c, k_s, v_s, k_w, v_w))

    qg = q.reshape(B, T, G, Hg, dh)
    kc = compress_tokens(k_c, cmp_pos[0], cmp_w1[0], cmp_b1[0], cmp_w2[0], cmp_b2[0])
    vc = compress_tokens(v_c, cmp_pos[1], cmp_w1[1], cmp_b1[1], cmp_w2[1], cmp_b2[1])
    n_cmp = kc.shape[1]
    c_start = jnp.arange(n_cmp) * CMP_STRIDE
    s_c = jnp.einsum('btghd,bcgd->bghtc', qg, kc) * scale
    p_c = masked_softmax(s_c, (c_start + CMP_BLOCK - 1)[None, :] <= t_idx[:, None])
    o_cmp = jnp.einsum('bghtc,bcgd->btghd', p_c.astype(vc.dtype), vc)

    n_blk = T // SEL_BLOCK
    s_start = jnp.arange(n_blk) * SEL_BLOCK
    overlap = ((c_start[:, None] <= s_start[None, :] + SEL_BLOCK - 1)
               & (c_start[:, None] + CMP_BLOCK - 1 >= s_start[None, :])).astype(jnp.float32)
    imp = jnp.einsum('bghtc,cs->bgts', p_c, overlap)
    cur = t_idx // SEL_BLOCK
    blk = jnp.arange(n_blk)
    valid = blk[None, :] <= cur[:, None]
    dist = cur[:, None] - blk[None, :]
    forced = (blk[None, :] == 0) | ((dist >= 0) & (dist < N_LOCAL_SEL))
    imp = jnp.where(forced, FORCED_SCORE, jnp.where(valid, imp, -1.0))
    n_sel = min(N_SELECT, n_blk)
    _, sel_idx = lax.top_k(imp, n_sel)

    q_r = partial_rope(q.reshape(B, T, NSA_HEADS, dh), positions).reshape(B, T, G, Hg, dh)
    k_s = partial_rope(k_s, positions)
    k_w = partial_rope(k_w, positions)

    k_blocks = k_s.reshape(B, n_blk, SEL_BLOCK, G, dh).transpose(0, 3, 1, 2, 4)
    v_blocks = v_s.reshape(B, n_blk, SEL_BLOCK, G, dh).transpose(0, 3, 1, 2, 4)
    b_ix = jnp.arange(B)[:, None, None, None]
    g_ix = jnp.arange(G)[None, :, None, None]
    n_keys_sel = n_sel * SEL_BLOCK

    def sel_chunk(ci):
        s0 = ci * SEL_Q_CHUNK
        qc = lax.dynamic_slice_in_dim(q_r, s0, SEL_Q_CHUNK, axis=1)
        ic = lax.dynamic_slice_in_dim(sel_idx, s0, SEL_Q_CHUNK, axis=2)
        kg = k_blocks[b_ix, g_ix, ic].reshape(B, G, SEL_Q_CHUNK, n_keys_sel, dh)
        vg = v_blocks[b_ix, g_ix, ic].reshape(B, G, SEL_Q_CHUNK, n_keys_sel, dh)
        kpos = (ic[..., None] * SEL_BLOCK + jnp.arange(SEL_BLOCK)).reshape(B, G, SEL_Q_CHUNK, n_keys_sel)
        qpos = s0 + jnp.arange(SEL_Q_CHUNK)
        s = jnp.einsum('bqghd,bgqkd->bghqk', qc, kg) * scale
        p = masked_softmax(s, (kpos <= qpos[None, None, :, None])[:, :, None])
        return jnp.einsum('bghqk,bgqkd->bqghd', p.astype(vg.dtype), vg)

    o_slc = lax.map(sel_chunk, jnp.arange(T // SEL_Q_CHUNK))
    o_slc = jnp.moveaxis(o_slc, 0, 1).reshape(B, T, G, Hg, dh)

    k_pad = jnp.pad(k_w, ((0, 0), (WINDOW, 0), (0, 0), (0, 0)))
    v_pad = jnp.pad(v_w, ((0, 0), (WINDOW, 0), (0, 0), (0, 0)))
    band = WINDOW + WIN_Q_BLOCK

    def win_block(bi):
        s0 = bi * WIN_Q_BLOCK
        qb = lax.dynamic_slice_in_dim(q_r, s0, WIN_Q_BLOCK, axis=1)
        kb = lax.dynamic_slice_in_dim(k_pad, s0, band, axis=1)
        vb = lax.dynamic_slice_in_dim(v_pad, s0, band, axis=1)
        kpos = s0 - WINDOW + jnp.arange(band)
        qpos = s0 + jnp.arange(WIN_Q_BLOCK)
        mask = ((kpos[None, :] <= qpos[:, None]) & (kpos[None, :] > qpos[:, None] - WINDOW)
                & (kpos[None, :] >= 0))
        s = jnp.einsum('bqghd,bkgd->bghqk', qb, kb) * scale
        p = masked_softmax(s, mask)
        return jnp.einsum('bghqk,bkgd->bqghd', p.astype(vb.dtype), vb)

    o_win = lax.map(win_block, jnp.arange(T // WIN_Q_BLOCK))
    o_win = jnp.moveaxis(o_win, 0, 1).reshape(B, T, G, Hg, dh)

    g = jax.nn.sigmoid(gate_logits).reshape(B, T, G, Hg, 3)
    out = g[..., 0:1] * o_cmp + g[..., 1:2] * o_slc + g[..., 2:3] * o_win
    return out.reshape(B, T, NSA_WIDTH)

def memory_attention(hn, mem_n, w_q, w_k, w_v, w_o):
    B, T, D = hn.shape
    M = mem_n.shape[1]
    q = (hn @ w_q).reshape(B, T, MEM_HEADS, MEM_HEAD_DIM)
    k = (mem_n @ w_k).reshape(B, M, MEM_HEADS, MEM_HEAD_DIM)
    v = (mem_n @ w_v).reshape(B, M, MEM_HEADS, MEM_HEAD_DIM)
    s = jnp.einsum('bthd,bmhd->bhtm', q, k).astype(jnp.float32) * (MEM_HEAD_DIM ** -0.5)
    p = jax.nn.softmax(s, axis=-1).astype(v.dtype)
    o = jnp.einsum('bhtm,bmhd->bthd', p, v).reshape(B, T, D)
    return o @ w_o

def peer(hn, w_q, sub_keys, u_emb, v_emb):
    B, T, D = hn.shape
    q = (hn @ w_q).reshape(B, T, PEER_HEADS, 2, PEER_HALF)
    s = jnp.einsum('bthpd,hpkd->bthpk', q, sub_keys).astype(jnp.float32)
    s_top, i_top = lax.top_k(s, PEER_TOPK)
    cand = s_top[..., 0, :, None] + s_top[..., 1, None, :]
    cand_idx = i_top[..., 0, :, None] * PEER_KEYS + i_top[..., 1, None, :]
    n_cand = PEER_TOPK * PEER_TOPK
    best, pos = lax.top_k(cand.reshape(B, T, PEER_HEADS, n_cand), PEER_TOPK)
    experts = jnp.take_along_axis(cand_idx.reshape(B, T, PEER_HEADS, n_cand), pos, axis=-1)
    gates = jax.nn.softmax(best, axis=-1).astype(hn.dtype)
    n_tok = B * T
    n_ret = PEER_HEADS * PEER_TOPK
    xs = hn.reshape(n_tok // PEER_TOKEN_CHUNK, PEER_TOKEN_CHUNK, D)
    es = experts.reshape(n_tok // PEER_TOKEN_CHUNK, PEER_TOKEN_CHUNK, n_ret)
    gs = gates.reshape(n_tok // PEER_TOKEN_CHUNK, PEER_TOKEN_CHUNK, n_ret)

    def chunk(args):
        xc, ec, gc = args
        u = u_emb[ec]
        a = jax.nn.gelu(jnp.einsum('nd,nkd->nk', xc, u))
        return jnp.einsum('nk,nkd->nd', gc * a, v_emb[ec])

    y = lax.map(chunk, (xs, es, gs))
    return y.reshape(B, T, D)

def second_inputs(seed: int = 0) -> dict:
    key = jax.random.key(seed)
    ks = jax.random.split(key, 32)
    L, D = DEPTH_2, D_MODEL
    nrm = lambda k, shape, sc: jax.random.normal(k, shape, jnp.float32) * sc
    gain = lambda k, shape: 1.0 + 0.02 * jax.random.normal(k, shape, jnp.float32)
    return {
        "x": nrm(ks[0], (BATCH, SEQ, D), 1.0),
        "mem": nrm(ks[1], (BATCH, MEM_LEN, D), 1.0),
        "positions": jnp.broadcast_to(jnp.arange(SEQ, dtype=jnp.int32), (BATCH, SEQ)),
        "mix_norm_g": gain(ks[2], (L, D)),
        "w_in": nrm(ks[3], (L, D, IN_COLS), D ** -0.5),
        "conv_dw_w": nrm(ks[4], (L, CONV_KERNEL, CONV_WIDTH_2), CONV_KERNEL ** -0.5),
        "conv_dw_b": nrm(ks[5], (L, CONV_WIDTH_2), 0.02),
        "conv_ln_g": gain(ks[6], (L, CONV_WIDTH_2)),
        "conv_ln_b": nrm(ks[7], (L, CONV_WIDTH_2), 0.02),
        "cmp_pos": nrm(ks[8], (L, 2, CMP_BLOCK, HEAD_DIM), 0.02),
        "cmp_w1": nrm(ks[9], (L, 2, CMP_BLOCK * HEAD_DIM, CMP_HIDDEN), (CMP_BLOCK * HEAD_DIM) ** -0.5),
        "cmp_b1": nrm(ks[10], (L, 2, CMP_HIDDEN), 0.02),
        "cmp_w2": nrm(ks[11], (L, 2, CMP_HIDDEN, HEAD_DIM), CMP_HIDDEN ** -0.5),
        "cmp_b2": nrm(ks[12], (L, 2, HEAD_DIM), 0.02),
        "w_out": nrm(ks[13], (L, MIX_WIDTH, D), MIX_WIDTH ** -0.5),
        "mem_q_norm_g": gain(ks[14], (L, D)),
        "mem_kv_norm_g": gain(ks[15], (L, D)),
        "w_mem_q": nrm(ks[16], (L, D, D), D ** -0.5),
        "w_mem_k": nrm(ks[17], (L, D, D), D ** -0.5),
        "w_mem_v": nrm(ks[18], (L, D, D), D ** -0.5),
        "w_mem_o": nrm(ks[19], (L, D, D), D ** -0.5),
        "peer_norm_g": gain(ks[20], (L, D)),
        "peer_w_q": nrm(ks[21], (L, D, PEER_HEADS * PEER_QDIM), D ** -0.5),
        "peer_sub_keys": nrm(ks[22], (L, PEER_HEADS, 2, PEER_KEYS, PEER_HALF), PEER_HALF ** -0.5),
        "peer_u": nrm(ks[23], (L, PEER_EXPERTS, D), D ** -0.5),
        "peer_v": nrm(ks[24], (L, PEER_EXPERTS, D), D ** -0.5),
        "final_norm_g": gain(ks[25], (D,)),
    }

def second_block(x, mem, positions, mix_norm_g, w_in, conv_dw_w, conv_dw_b, conv_ln_g, conv_ln_b,
              cmp_pos, cmp_w1, cmp_b1, cmp_w2, cmp_b2, w_out,
              mem_q_norm_g, mem_kv_norm_g, w_mem_q, w_mem_k, w_mem_v, w_mem_o,
              peer_norm_g, peer_w_q, peer_sub_keys, peer_u, peer_v, final_norm_g):
    h = x
    for l in range(DEPTH_2):
        hn = rmsnorm(h, mix_norm_g[l])
        proj = hn @ w_in[l]
        conv_a, conv_b, q, k_c, v_c, k_s, v_s, k_w, v_w, gate_logits = jnp.split(proj, IN_SPLITS, axis=-1)
        y_conv = conformer_conv(conv_a, conv_b, conv_dw_w[l], conv_dw_b[l], conv_ln_g[l], conv_ln_b[l])
        y_nsa = nsa_mixer(q, k_c, v_c, k_s, v_s, k_w, v_w, gate_logits, positions,
                          cmp_pos[l], cmp_w1[l], cmp_b1[l], cmp_w2[l], cmp_b2[l])
        h = h + jnp.concatenate([y_conv, y_nsa], axis=-1) @ w_out[l]
        h = h + memory_attention(rmsnorm(h, mem_q_norm_g[l]), rmsnorm(mem, mem_kv_norm_g[l]),
                                 w_mem_q[l], w_mem_k[l], w_mem_v[l], w_mem_o[l])
        h = h + peer(rmsnorm(h, peer_norm_g[l]), peer_w_q[l], peer_sub_keys[l], peer_u[l], peer_v[l])
    return rmsnorm(h, final_norm_g)


def setup_inputs(seed=0):
    out = dict(first_inputs(seed))
    for name, value in second_inputs(seed + 1).items():
        if name != "x":
            out[name + "_2"] = value
    return out


def reference(
    x, g_ffn1, w_up1, w_down1, g_mix, w_in, b_gate, conv_w, conv_b, w_a, b_a, w_x, b_x, lam,
    g_q, g_k, b_forget, w_lru_out, w_attn_out, w_o, g_ffn2, w_up2, w_down2, mem_2, positions_2,
    mix_norm_g_2, w_in_2, conv_dw_w_2, conv_dw_b_2, conv_ln_g_2, conv_ln_b_2, cmp_pos_2,
    cmp_w1_2, cmp_b1_2, cmp_w2_2, cmp_b2_2, w_out_2, mem_q_norm_g_2, mem_kv_norm_g_2, w_mem_q_2,
    w_mem_k_2, w_mem_v_2, w_mem_o_2, peer_norm_g_2, peer_w_q_2, peer_sub_keys_2, peer_u_2,
    peer_v_2, final_norm_g_2,
):
    x = first_block(
        x, g_ffn1, w_up1, w_down1, g_mix, w_in, b_gate, conv_w, conv_b, w_a, b_a, w_x, b_x, lam,
        g_q, g_k, b_forget, w_lru_out, w_attn_out, w_o, g_ffn2, w_up2, w_down2,
    )
    return second_block(
        x, mem_2, positions_2, mix_norm_g_2, w_in_2, conv_dw_w_2, conv_dw_b_2, conv_ln_g_2,
        conv_ln_b_2, cmp_pos_2, cmp_w1_2, cmp_b1_2, cmp_w2_2, cmp_b2_2, w_out_2, mem_q_norm_g_2,
        mem_kv_norm_g_2, w_mem_q_2, w_mem_k_2, w_mem_v_2, w_mem_o_2, peer_norm_g_2, peer_w_q_2,
        peer_sub_keys_2, peer_u_2, peer_v_2, final_norm_g_2,
    )


_drawn_inputs = setup_inputs


def setup_inputs(seed=0):
    import zlib

    import numpy as np

    out = dict(_drawn_inputs(seed))
    spreads = {}
    factors = {'g_ffn1': 4.264,
     'g_mix': 4.881,
     'b_gate': 8.0,
     'b_a': 8.0,
     'b_x': 8.0,
     'g_q': 8.0,
     'g_k': 8.0,
     'g_ffn2': 5.128,
     'mix_norm_g_2': 7.314,
     'conv_dw_b_2': 4.234,
     'conv_ln_g_2': 7.425,
     'conv_ln_b_2': 8.0,
     'cmp_pos_2': 8.0,
     'cmp_b1_2': 8.0,
     'cmp_b2_2': 8.0,
     'mem_q_norm_g_2': 8.0,
     'mem_kv_norm_g_2': 8.0,
     'peer_norm_g_2': 8.0,
     'peer_w_q_2': 4.932,
     'peer_sub_keys_2': 4.938,
     'peer_u_2': 5.479,
     'peer_v_2': 4.963,
     'final_norm_g_2': 2.819}
    for name, (base, spread) in spreads.items():
        noise = np.random.default_rng([zlib.crc32(name.encode()), seed]).standard_normal(out[name].shape)
        drawn = base * np.exp(spread * noise) if base else spread * noise
        out[name] = __import__('jax').numpy.asarray(drawn.astype(out[name].dtype))
    for name, factor in factors.items():
        out[name] = (out[name] * factor).astype(out[name].dtype)
    return out
```

```python
import numpy as np
import concourse.bass as bass
from concourse import mybir
from contextlib import ExitStack

F32 = mybir.dt.float32
F32R = mybir.dt.float32r
U32 = mybir.dt.uint32
I32 = mybir.dt.int32
ACT = mybir.ActivationFunctionType
ALU = mybir.AluOpType
AX = mybir.AxisListType

P = 128
D = 1024
S = 512
DC = D // P
LAYERS = 2
F_FF = 2816
FC = F_FF // P
HEADS = 16
HD = 64
EPS = 1e-6
TILE = 2048
QB = S // P
NEG = -1e30

PRM = {}
for _n, _w in (("g_ffn1", 8), ("g_mix", 8), ("g_ffn2", 8), ("b_gate", 16), ("conv_w", 32), ("conv_b", 8),
               ("b_a", 8), ("b_x", 8), ("lam", 8), ("b_f", 1), ("g_q", 1), ("g_k", 1)):
    PRM[_n] = (sum(w for _, w in PRM.values()), _w)
NPRM = sum(w for _, w in PRM.values())

LAYER_TILES = (("up", 22), ("down", 11), ("lx", 4), ("lg", 1), ("wax", 1), ("lg", 3), ("lru", 8), ("f", 1), ("v", 4),
               ("qk", 8), ("attn", 8), ("wo", 4), ("up", 22), ("down", 11))
TL = sum(n for _, n in LAYER_TILES)
TL_PAD = TL % 2
TL += TL_PAD


PN_LAYER = 22 + 4 + 4 + 8 + 8 + 4 + 2 + 8 + 8 + 4 + 22
PHASES_LAYER = 5


class Cursor:

    def __init__(self):
        self.base_q, self.base_n, self.base_ph = 0, 0, 0
        self.t, self.n, self.ph = 0, 0, 0

    def enter_layer(self, layer):
        self.base_q, self.base_n, self.base_ph = layer * (TL // 2), layer * PN_LAYER, layer * PHASES_LAYER
        self.t, self.n, self.ph = 0, 0, 0

    def leave_layers(self):
        assert (self.t, self.n, self.ph) == (TL, PN_LAYER, PHASES_LAYER), (self.t, self.n, self.ph)
        self.enter_layer(LAYERS)


class Tile:

    def __init__(self, cur, i, j, pairs):
        self.i, self.j = i, j
        self.k = i * 2 + j
        self.p = (cur.t + j) % 2
        self.t = cur.base_q * 2 + i * 2 + (cur.t + j)
        self.loads = cur.base_q + i + (cur.t + j) // 2
        self.next_p = 1 - self.p
        self.next_loads = cur.base_q + i + (cur.t + j + 1) // 2
        self.n = cur.base_n + i * (2 * pairs) + (cur.n + pairs * j)
        self.b = 2 * ((cur.n + pairs * j) % 2)


def one_tile(cur):
    tile = Tile(cur, 0, 0, 1)
    cur.t += 1
    cur.n += 1
    return tile


def tiles(eng, cur, count, pairs=1):
    half = count // 2
    if half > 1:
        with eng.Fori(0, half) as i:
            for j in (0, 1):
                yield Tile(cur, i, j, pairs)
    elif half:
        for j in (0, 1):
            yield Tile(cur, 0, j, pairs)
    if count % 2:
        yield Tile(cur, 0, count - 1, pairs)
    cur.t += count
    cur.n += count * pairs


class Ctx:

    def __init__(self, nc, stack):
        self.nc, self.stack, self.sems = nc, stack, {}

    def sb(self, name, shape, dt=F32, stack=None):
        return (stack or self.stack).enter_context(self.nc.sbuf_tensor(name, shape, dt))

    def sem(self, name):
        if name not in self.sems:
            self.sems[name] = self.stack.enter_context(self.nc.semaphore(name))
        return self.sems[name]


def phase_end(c, eng, cur):
    eng.drain().then_inc(c.sem("phase_done"), 1)
    cur.ph += 1
    eng.wait_ge(c.sem("phase_done"), cur.base_ph * 3 + 3 * cur.ph)
    carry_wait(c, eng)


def carry_wait(c, eng):
    eng.sem_inc(c.sem("wait_carried"), 1)



def sp_weight_loads(c, sp, stream, first, count):
    def load(t, p, loads, wait):
        if wait:
            sp.wait_ge(c.sem("w_split"), t - 1)
        sp.dma_start(c.RAW[p][:, :], stream(t)).then_inc(c.sem(f"w_loaded{p}"), 16)
    half = count // 2
    start = 0
    if first == 0:
        load(0, 0, 0, False)
        load(1, 1, 0, False)
        start = 1
    if half > start:
        with sp.Fori(start, half) as i:
            load(first + i * 2, 0, None, True)
            load(first + i * 2 + 1, 1, None, True)
    if count % 2:
        load(first + count - 1, (first + count - 1) % 2, None, True)


def act_split(c, act, t, p, loads):
    act.wait_ge(c.sem(f"w_loaded{p}"), loads * 16 + 16)
    act.wait_ge(c.sem("tile_done"), t + 1)
    c.nc.scalar.activation(c.WH[p][:, :], c.RAW[p][:, :], ACT.Copy).then_inc(c.sem("w_hi"), 1)


def dve_split(c, dve, t, p):
    dve.wait_ge(c.sem("w_hi"), t + 1)
    c.nc.vector.tensor_tensor(c.WL[p][:, :], c.RAW[p][:, :], c.WH[p][:, :].bitcast(F32),
                              ALU.subtract).then_inc(c.sem("w_split"), 1)


def act_next(c, act, tile):
    act_split(c, act, tile.t + 1, tile.next_p, tile.next_loads)


def dve_next(c, dve, tile):
    dve_split(c, dve, tile.t + 1, tile.next_p)


def mm3(c, out, wh, wl, xh, xl, start, stop):
    c.nc.tensor.matmul(out, wh, xh, start=start, stop=False)
    c.nc.tensor.matmul(out, wh, xl, start=False, stop=False)
    return c.nc.tensor.matmul(out, wl, xh, start=False, stop=stop)


def pe_pair_tile(c, pe, tile, XH, XL, width=S):
    pe.wait_ge(c.sem("w_split"), tile.t + 1)
    pe.wait_ge(c.sem("ps_done"), tile.n + 1)
    WH = c.WH[tile.p][:, :].rearrange("p (k m c) -> p k m c", k=DC, m=2)
    WL = c.WL[tile.p][:, :].rearrange("p (k m c) -> p k m c", k=DC, m=2)
    for m in range(2):
        for k in range(DC):
            last = mm3(c, c.PB[:, tile.b + m, :width], WH[:, k, m, :], WL[:, k, m, :],
                       XH[:, k, :width], XL[:, k, :width], k == 0, k == DC - 1)
    last.then_inc(c.sem("tile_done"), 1)



def act_norm(c, act, v, X, XH, width=S, bank=4, news=None):
    SQ = c.SQ
    for k in range(0, DC, 2):
        if news is not None:
            act.wait_ge(c.sem("x_new"), news + k // 2 + 1)
        c.nc.scalar.activation(SQ[:, k:k + 2, :width], X[:, k:k + 2, :width], ACT.Square)\
            .then_inc(c.sem("sq_ready"), 1)
    act.wait_ge(c.sem("norm_sum"), v + 1)
    c.nc.scalar.activation(c.RS[:, :width], c.PB[:, bank, :width], ACT.Sqrt, bias=c.EPSC[:, 0:1], scale=1.0 / D)\
        .then_inc(c.sem("norm_root"), 1)
    for k in range(DC if XH is not None else 0):
        act.wait_ge(c.sem("xn_ready"), v * DC + k + 1)
        c.nc.scalar.activation(XH[:, k, :width], c.PB[:, 6 + k % 2, :width], ACT.Copy).then_inc(c.sem("xn_hi"), 1)


def pe_norm(c, pe, v, width=S, bank=4):
    for k in range(DC):
        if k % 2 == 0:
            pe.wait_ge(c.sem("sq_ready"), v * 4 + k // 2 + 1)
        last = c.nc.tensor.matmul(c.PB[:, bank, :width], c.ONES[:, :], c.SQ[:, k, :width],
                                  start=(k == 0), stop=(k == DC - 1))
    last.then_inc(c.sem("norm_sum"), 1)


def pe_normed_tile(c, pe, cur, v, width=S):
    tile = one_tile(cur)
    pe.wait_ge(c.sem("w_split"), tile.t + 1)
    pe.wait_ge(c.sem("ps_done"), tile.n + 1)
    WH = c.WH[tile.p][:, :].rearrange("p (k m c) -> p k m c", k=DC, m=2)
    WL = c.WL[tile.p][:, :].rearrange("p (k m c) -> p k m c", k=DC, m=2)
    for k in range(DC):
        pe.wait_ge(c.sem("xn_lo"), v * DC + k + 1)
        for m in range(2):
            last = mm3(c, c.PB[:, tile.b + m, :width], WH[:, k, m, :], WL[:, k, m, :],
                       c.XH[:, k, :width], c.XL[:, k, :width], k == 0, k == DC - 1)
    last.then_inc(c.sem("tile_done"), 1)


def dve_norm(c, dve, v, X, g, XH, XL, width=S, out=None):
    V = c.nc.vector
    dve.wait_ge(c.sem("norm_root"), v + 1)
    V.reciprocal(c.PB[:, 5, :width], c.RS[:, :width])
    dve.drain()

    def low(k):
        dve.wait_ge(c.sem("xn_hi"), v * DC + k + 1)
        V.tensor_tensor(XL[:, k, :width], c.PB[:, 6 + k % 2, :width], XH[:, k, :width].bitcast(F32),
                        ALU.subtract).then_inc(c.sem("xn_lo"), 1)
    for k in range(DC):
        dst = c.PB[:, 6 + k % 2, :width] if out is None else out[:, k, :width]
        V.scalar_tensor_tensor(out=dst, in0=X[:, k, :width], scalar=g(k), in1=c.PB[:, 5, :width],
                               op0=ALU.mult, op1=ALU.mult).then_inc(c.sem("xn_ready"), 1)
        if out is None and k:
            low(k - 1)
            dve.drain()
    if out is None:
        low(DC - 1)



def pe_ffn(c, pe, cur, v, norm):
    pe_normed_tile(c, pe, cur, norm)
    for tile in tiles(pe, cur, FC - 1):
        pe_pair_tile(c, pe, tile, c.XH, c.XL)
    phase_end(c, pe, cur)
    for tile, k0 in down_tiles(pe, cur):
        pe.wait_ge(c.sem("w_split"), tile.t + 1)
        WH = c.WH[tile.p][:, :].rearrange("p (k m c) -> p k m c", k=2, m=DC)
        WL = c.WL[tile.p][:, :].rearrange("p (k m c) -> p k m c", k=2, m=DC)
        for kk in range(2):
            first = k0 == 0 and kk == 0
            for m in range(DC):
                last = mm3(c, c.PB[:, m, :], WH[:, kk, m, :], WL[:, kk, m, :],
                           c.HH[:, tile.k * 2 + kk, :], c.HL[:, tile.k * 2 + kk, :],
                           first, k0 == FC // 2 - 1 and kk == 1)
        last.then_inc(c.sem("tile_done"), 1)


def down_tiles(eng, cur):
    yield Tile(cur, 0, 0, 0), 0
    cur.t += 1
    with eng.Fori(0, (FC // 2 - 3) // 2) as i:
        for j in (0, 1):
            tile = Tile(cur, i, j, 0)
            tile.k = i * 2 + j + 1
            yield tile, None
    cur.t += FC // 2 - 3
    for k in (FC // 2 - 2, FC // 2 - 1):
        tile = Tile(cur, 0, 0, 0)
        tile.k = k
        yield tile, k
        cur.t += 1


def act_ffn(c, act, cur, v):
    for tile in tiles(act, cur, FC):
        act_next(c, act, tile)
        act.wait_ge(c.sem("tile_done"), tile.t + 3)
        s = tile.b // 2
        c.nc.scalar.activation(c.SIL[:, s, :], c.PB[:, tile.b, :], ACT.Silu).then_inc(c.sem("silu"), 1)
        act.wait_ge(c.sem("ps_done"), tile.n + 3)
        c.nc.scalar.activation(c.HH[:, tile.k, :], c.PROD[:, s, :], ACT.Copy).then_inc(c.sem("h_hi"), 1)
    phase_end(c, act, cur)
    for tile, _ in down_tiles(act, cur):
        act_next(c, act, tile)
    act.wait_ge(c.sem("tile_done"), tile.t + 3)


def dve_ffn(c, dve, cur, v):
    base = v * FC
    for tile in tiles(dve, cur, FC):
        dve_next(c, dve, tile)
        s = tile.b // 2
        dve.wait_ge(c.sem("silu"), base + tile.k + 1)
        c.nc.vector.tensor_tensor(c.PROD[:, s, :], c.SIL[:, s, :], c.PB[:, tile.b + 1, :], ALU.mult)\
            .then_inc(c.sem("ps_done"), 1)
        dve.wait_ge(c.sem("h_hi"), base + tile.k + 1)
        c.nc.vector.tensor_tensor(c.HL[:, tile.k, :], c.PROD[:, s, :], c.HH[:, tile.k, :].bitcast(F32),
                                  ALU.subtract)
    phase_end(c, dve, cur)
    for tile, _ in down_tiles(dve, cur):
        dve_next(c, dve, tile)
    dve.wait_ge(c.sem("tile_done"), tile.t + 3)
    for m in range(0, DC, 2):
        xs = c.X[:, m:m + 2, :]
        c.nc.vector.scalar_tensor_tensor(out=xs, in0=c.PB[:, m:m + 2, :], scalar=0.5, in1=xs,
                                         op0=ALU.mult, op1=ALU.add).then_inc(c.sem("x_new"), 1)



def wax_pairs(cur):
    for k in range(DC):
        yield k, cur.base_n + (cur.n + k), 2 * ((cur.n + k) % 2)


def pe_lru(c, pe, cur, l):
    pe_normed_tile(c, pe, cur, l * 3 + 1)
    for tile in tiles(pe, cur, 3):
        pe_pair_tile(c, pe, tile, c.XH, c.XL)
    pe_pair_tile(c, pe, one_tile(cur), c.XH, c.XL)
    for tile in tiles(pe, cur, 1, 0):
        pe.wait_ge(c.sem("w_split"), tile.t + 1)
        WH = c.WH[tile.p][:, :].rearrange("p (g k c) -> p g k c", g=2, k=DC)
        WL = c.WL[tile.p][:, :].rearrange("p (g k c) -> p g k c", g=2, k=DC)
        for k, n, b in wax_pairs(cur):
            if k % 2 == 0:
                pe.wait_ge(c.sem("conv_lo"), l * 4 + k // 2 + 1)
            pe.wait_ge(c.sem("ps_done"), n + 1)
            for g in range(2):
                last = mm3(c, c.PB[:, b + g, :], WH[:, g, k, :], WL[:, g, k, :], c.YH[:, k, :], c.YL[:, k, :],
                           True, True)
            if k < DC - 1:
                last.then_inc(c.sem("gates_full"), 1)
        last.then_inc(c.sem("tile_done"), 1)
    cur.n += DC
    for tile in tiles(pe, cur, 3):
        pe_pair_tile(c, pe, tile, c.XH, c.XL)
    pe_gated_lru(c, pe, cur, l)


def act_lru(c, act, cur, l):
    A = c.nc.scalar
    base = l * DC

    def gelu(tile, at):
        act.wait_ge(c.sem("tile_done"), tile.t + 3)
        act.wait_ge(c.sem("ps_done"), tile.n + 2)
        A.activation(c.LG[:, at:at + 2, :], c.PB[:, tile.b:tile.b + 2, :], ACT.Gelu_apprx_tanh)\
            .then_inc(c.sem("ps_done"), 1)

    def decay(k):
        if k >= 2:
            act.wait_ge(c.sem("one_less"), base + k - 1)
        A.activation(c.PB[:, 6 + k % 2, :], c.AA[:, k, :], ACT.Tanh, scale=c.SPP[:, l, k:k + 1])
        A.activation(c.ZX[:, k, :], c.AA[:, k, :], ACT.Exp, scale=c.SPN2[:, l, k:k + 1])
        act.drain()
        A.activation(c.AA[:, k, :], c.AA[:, k, :], ACT.Exp, scale=c.SPN[:, l, k:k + 1]).then_inc(c.sem("decay"), 1)

    def root(k):
        act.wait_ge(c.sem("one_less"), base + k + 1)
        if k >= 2:
            act.wait_ge(c.sem("scanned"), base + k - 1)
        A.activation(c.PB[:, 4 + k % 2, :], c.ZX[:, k, :], ACT.Sqrt).then_inc(c.sem("lru_root"), 1)

    for tile in tiles(act, cur, 4):
        act_next(c, act, tile)
        act.wait_ge(c.sem("conv_out"), l * 4 + tile.k + 1)
        A.activation(c.YH[:, bass.ds(tile.k * 2, 2), :], c.XR[:, bass.ds(tile.k * 2, 2), :], ACT.Copy)\
            .then_inc(c.sem("conv_hi"), 1)
    tile = one_tile(cur)
    act_next(c, act, tile)
    gelu(tile, 0)
    for tile in tiles(act, cur, 1, 0):
        act_next(c, act, tile)
        for k, n, b in wax_pairs(cur):
            if k < DC - 1:
                act.wait_ge(c.sem("gates_full"), l * (DC - 1) + k + 1)
            else:
                act.wait_ge(c.sem("tile_done"), tile.t + 3)
            if k >= 2:
                act.wait_ge(c.sem("x_gated"), base + k - 1)
            col = PRM["b_a"][0] + k
            A.activation(c.AA[:, k, :], c.PB[:, b, :], ACT.Sigmoid, bias=c.PR[:, l, col:col + 1])
            col = PRM["b_x"][0] + k
            A.activation(c.PB[:, 4 + k % 2, :], c.PB[:, b + 1, :], ACT.Sigmoid, bias=c.PR[:, l, col:col + 1])\
                .then_inc(c.sem("ps_done"), 1)
    cur.n += DC
    for j in range(3):
        tile = one_tile(cur)
        act_next(c, act, tile)
        for k in ((0, 1, 2, 3), (4, 5, 6, 7), ())[j]:
            decay(k)
        for k in ((), (0, 1, 2), (3, 4, 5, 6))[j]:
            root(k)
        gelu(tile, 2 * j + 2)
    for j in range(2):
        tile = one_tile(cur)
        act_next(c, act, tile)
        if j == 0:
            root(DC - 1)
        for k in ((0, 1, 2, 3, 4, 5), (6, 7))[j]:
            act.wait_ge(c.sem("lru_y"), base + k + 1)
            A.activation(c.YH[:, k, :], c.PB[:, 6 + k % 2, :], ACT.Copy).then_inc(c.sem("y_hi"), 1)
        act_gate(c, act, tile, l, 0, j, j * 2)
    for j in range(2):
        act_next(c, act, one_tile(cur))
    for j in range(4):
        tile = one_tile(cur)
        act_next(c, act, tile)
        if j < 2:
            act_gate(c, act, tile, l, 0, j, 4 + j * 2)
    phase_end(c, act, cur)


def dve_lru(c, dve, cur, l):
    V = c.nc.vector
    base = l * DC
    w, b = PRM["conv_w"][0], PRM["conv_b"][0]
    for tile in tiles(dve, cur, 4):
        dve_next(c, dve, tile)
        dve.wait_ge(c.sem("tile_done"), tile.t + 3)
        for m in range(2):
            V.tensor_scalar(c.XR[:, bass.ds(tile.k * 2 + m, 1), :].rearrange("p a s -> p (a s)"),
                            c.PB[:, tile.b + m, :],
                            c.PR[:, l, bass.ds(tile.k * 8 + (w + 4 * m + 3), 1)],
                            c.PR[:, l, bass.ds(tile.k * 2 + (b + m), 1)], ALU.mult, ALU.add)
        dve.drain()
        for back in (1, 2, 3):
            for m in range(2):
                out = c.XR[:, bass.ds(tile.k * 2 + m, 1), back:].rearrange("p a s -> p (a s)")
                last = V.scalar_tensor_tensor(out=out, in0=c.PB[:, tile.b + m, :S - back],
                                              scalar=c.PR[:, l, bass.ds(tile.k * 8 + (w + 4 * m + 3 - back), 1)],
                                              in1=out, op0=ALU.mult, op1=ALU.add)
            if back < 3:
                dve.drain()
        last.then_inc(c.sem("ps_done"), 1)
        dve.drain().then_inc(c.sem("conv_out"), 1)
    tile = one_tile(cur)
    dve_next(c, dve, tile)
    dve.wait_ge(c.sem("conv_hi"), l * 4 + 4)
    for k in range(0, DC, 2):
        V.tensor_tensor(c.YL[:, k:k + 2, :], c.XR[:, k:k + 2, :], c.YH[:, k:k + 2, :].bitcast(F32), ALU.subtract)\
            .then_inc(c.sem("conv_lo"), 1)
    for tile in tiles(dve, cur, 1, 0):
        dve_next(c, dve, tile)
        for k, n, b in wax_pairs(cur):
            dve.wait_ge(c.sem("ps_done"), n + 3)
            V.tensor_tensor(c.XR[:, k, :], c.XR[:, k, :], c.PB[:, 4 + k % 2, :], ALU.mult)\
                .then_inc(c.sem("x_gated"), 1)
    cur.n += DC

    def one_less(k):
        dve.wait_ge(c.sem("decay"), base + k + 1)
        V.scalar_tensor_tensor(out=c.ZX[:, k, :], in0=c.ZX[:, k, :], scalar=1.0, in1=c.PB[:, 6 + k % 2, :],
                               op0=ALU.add, op1=ALU.mult).then_inc(c.sem("one_less"), 1)

    def scan(k):
        dve.wait_ge(c.sem("lru_root"), base + k + 1)
        V.tensor_tensor(c.XR[:, k, :], c.XR[:, k, :], c.PB[:, 4 + k % 2, :], ALU.mult).then_inc(c.sem("scanned"), 1)
        dve.drain()
        V.tensor_tensor_scan(c.ZX[:, k, :], c.AA[:, k, :], c.XR[:, k, :], 0.0, ALU.mult, ALU.add)

    def low(k):
        dve.wait_ge(c.sem("y_hi"), base + k + 1)
        return V.tensor_tensor(c.YL[:, k, :], c.PB[:, 6 + k % 2, :], c.YH[:, k, :].bitcast(F32), ALU.subtract)

    for j in range(3):
        tile = one_tile(cur)
        dve_next(c, dve, tile)
        for k in ((0, 1, 2, 3), (4, 5, 6, 7), ())[j]:
            one_less(k)
        for k in ((), (0, 1), (2, 3, 4, 5, 6))[j]:
            scan(k)
    lg = tile
    for j in range(2):
        tile = one_tile(cur)
        dve_next(c, dve, tile)
        if j == 0:
            scan(DC - 1)
            dve.drain()
            dve.wait_ge(c.sem("ps_done"), lg.n + 3)
        for k in ((0, 1, 2, 3, 4, 5), (6, 7))[j]:
            V.tensor_tensor(c.PB[:, 6 + k % 2, :], c.ZX[:, k, :], c.LG[:, k, :], ALU.mult).then_inc(c.sem("lru_y"), 1)
            if k:
                low(k - 1)
                dve.drain()
    low(DC - 1).then_inc(c.sem("y_lo"), 1)
    for half in range(2):
        for j in range(4):
            if half or j >= 2:
                tile = one_tile(cur)
                dve_next(c, dve, tile)
                if j >= 2:
                    dve_gated_output(c, dve, tile, 0, j, half * 4 + (j - 2) * 2)
    phase_end(c, dve, cur)



def four_tiles(cur, i):
    for j in range(4):
        yield j, Tile(cur, i * 2, j, 1)


def pe_gated_lru(c, pe, cur, l):
    with pe.Fori(0, 2) as i:
        for j, tile in four_tiles(cur, i):
            if j < 2:
                pe_pair_tile(c, pe, tile, c.XH, c.XL)
            else:
                pe.wait_ge(c.sem("y_lo"), l + 1)
                pe_pair_tile(c, pe, tile, c.YH, c.YL)
    cur.t += 8
    cur.n += 8
    phase_end(c, pe, cur)


def pe_gated(c, pe, cur):
    for i in range(2):
        for j, tile in four_tiles(cur, i):
            if j >= 2:
                pe_pair_tile(c, pe, tile, c.YH, c.YL)
            elif i or j:
                pe_pair_tile(c, pe, tile, c.XH, c.XL)
    cur.t += 8
    cur.n += 8
    phase_end(c, pe, cur)


def act_gate(c, act, tile, l, branch, j, chunk):
    act.wait_ge(c.sem("tile_done"), tile.t + 3)
    act.wait_ge(c.sem("ps_done"), tile.n + 2)
    for m in range(2):
        at = chunk + (PRM["b_gate"][0] + branch * DC + m)
        last = c.nc.scalar.activation(c.SG[:, j * 2 + m, :], c.PB[:, tile.b + m, :], ACT.Sigmoid,
                                      bias=c.PR[:, l, bass.ds(at, 1)])
    last.then_inc(c.sem("ps_done"), 1)


def act_gated(c, act, cur, l):
    with act.Fori(0, 2) as i:
        for j, tile in four_tiles(cur, i):
            act_next(c, act, tile)
            if j < 2:
                act_gate(c, act, tile, l, 1, j, i * 4 + j * 2)
    cur.t += 8
    cur.n += 8
    for k in range(0, DC, 4):
        act.wait_ge(c.sem("mix_out"), l * 2 + (k // 4 + 1))
        c.nc.scalar.activation(c.MH[:, k:k + 4, :], c.M[:, k:k + 4, :], ACT.Copy).then_inc(c.sem("mix_hi"), 1)
    phase_end(c, act, cur)


def dve_gated_output(c, dve, tile, branch, j, chunk):
    V = c.nc.vector
    dve.wait_ge(c.sem("ps_done"), tile.n + 2)
    dve.wait_ge(c.sem("tile_done"), tile.t + 3)
    M = c.M[:, bass.ds(chunk, 2), :]
    gate = c.SG[:, (j - 2) * 2:(j - 2) * 2 + 2, :]
    if branch == 0:
        V.tensor_tensor(M, c.PB[:, tile.b:tile.b + 2, :], gate, ALU.mult).then_inc(c.sem("ps_done"), 1)
    else:
        part = c.SG2[:, (j - 2) * 2:(j - 2) * 2 + 2, :]
        V.tensor_tensor(part, c.PB[:, tile.b:tile.b + 2, :], gate, ALU.mult).then_inc(c.sem("ps_done"), 1)
        dve.drain()
        V.tensor_tensor(M, M, part, ALU.add)


def dve_gated(c, dve, cur, l):
    with dve.Fori(0, 2) as i:
        for j, tile in four_tiles(cur, i):
            dve_next(c, dve, tile)
            if j >= 2:
                dve_gated_output(c, dve, tile, 1, j, i * 4 + (j - 2) * 2)
        dve.drain().then_inc(c.sem("mix_out"), 1)
    cur.t += 8
    cur.n += 8
    for k in range(0, DC, 4):
        dve.wait_ge(c.sem("mix_hi"), l * 2 + (k // 4 + 1))
        c.nc.vector.tensor_tensor(c.ML[:, k:k + 4, :], c.M[:, k:k + 4, :], c.MH[:, k:k + 4, :].bitcast(F32),
                                  ALU.subtract)
    phase_end(c, dve, cur)




def pe_residual(c, pe, cur, YH, YL, phase=True):
    for tile in tiles(pe, cur, 4):
        pe_pair_tile(c, pe, tile, YH, YL)
    if phase:
        phase_end(c, pe, cur)


def act_residual(c, act, cur, phase=True):
    for tile in tiles(act, cur, 4):
        act_next(c, act, tile)
    if phase:
        phase_end(c, act, cur)


def dve_residual(c, dve, cur, phase=True):
    for tile in tiles(dve, cur, 4):
        dve_next(c, dve, tile)
        dve.wait_ge(c.sem("tile_done"), tile.t + 3)
        xs = c.X[:, bass.ds(tile.k * 2, 2), :]
        c.nc.vector.tensor_tensor(xs, xs, c.PB[:, tile.b:tile.b + 2, :], ALU.add).then_inc(c.sem("ps_done"), 1)
        if not phase:
            dve.drain().then_inc(c.sem("x_new"), 1)
    if phase:
        phase_end(c, dve, cur)



class Steps:

    def __init__(self, count, steps, bufs, sums=None):
        self.count, self.steps, self.sums = count, steps, sums
        self.PM, self.PT, self.SUM = bufs


def blocks(nk):
    return [(kb, min(P, nk - kb * P)) for kb in range((nk + P - 1) // P)]


def pe_steps(c, pe, st):
    def scores(j):
        if j < len(st.steps):
            pe.wait_ge(c.sem("p_ready"), st.count + (j + 1))
            st.steps[j]["scores"](c.PB[:, 6 + j % 2, :]).then_inc(c.sem("s_ready"), 1)

    def turn(j):
        pe.wait_ge(c.sem("p_ready"), st.count + (j + 3))
        pe.wait_ge(c.sem("pt_copied"), st.count + (j + 1))
        for kb, w in blocks(st.steps[j]["nk"]):
            last = c.nc.tensor.transpose(c.PB[:w, 4 + j % 2, kb * P:kb * P + P],
                                         st.PM[:, j % 2, kb * P:kb * P + w], c.IDENT[:, :])
        last.then_inc(c.sem("pt_ready"), 1)

    def product(j):
        step = st.steps[j]
        pe.wait_ge(c.sem("pt_copied"), st.count + (j + 3))
        if step["nk"] <= 32:
            carry_wait(c, pe)
        bl = blocks(step["nk"])
        for kb, w in bl:
            last = c.nc.tensor.matmul(step["out"], st.PT[:w, j % 2, kb * P:kb * P + P], step["values"](kb),
                                      start=kb == 0, stop=kb == len(bl) - 1)
        last.then_inc(c.sem("pv_done"), 1)

    scores(0)
    scores(1)
    turn(0)
    for j in range(len(st.steps)):
        scores(j + 2)
        if j + 1 < len(st.steps):
            turn(j + 1)
        product(j)


def dve_steps(c, dve, st):
    def top(j):
        if j < len(st.steps):
            dve.wait_ge(c.sem("s_ready"), st.count + (j + 1))
            nk = st.steps[j]["nk"]
            c.nc.vector.reduce_max(c.NM[:, j % 2:j % 2 + 1], c.PB[:, 6 + j % 2, :nk], axis=AX.X, negate=True)\
                .then_inc(c.sem("m_ready"), 1)

    def copy(j):
        dve.wait_ge(c.sem("pt_ready"), st.count + (j + 3))
        dve.wait_ge(c.sem("pv_done"), st.count + (j + 1))
        bl = blocks(st.steps[j]["nk"])
        w = bl[0][1]
        c.nc.vector.tensor_copy(st.PT[:w, j % 2, :len(bl) * P], c.PB[:w, 4 + j % 2, :len(bl) * P])\
            .then_inc(c.sem("pt_copied"), 1)

    top(0)
    top(1)
    copy(0)
    for j in range(len(st.steps)):
        top(j + 2)
        if j + 1 < len(st.steps):
            copy(j + 1)


def act_steps(c, act, st):
    for j, step in enumerate(st.steps):
        nk = step["nk"]
        act.wait_ge(c.sem("m_ready"), st.count + (j + 1))
        act.wait_ge(c.sem("pt_ready"), st.count + (j + 1))
        c.nc.scalar.activation(st.PM[:, j % 2, :nk], c.PB[:, 6 + j % 2, :nk], ACT.Exp,
                               bias=c.NM[:, j % 2:j % 2 + 1], scale=1.0, accum_out=st.SUM[:, st.sums[j]:st.sums[j] + 1])\
            .then_inc(c.sem("p_ready"), 1)


PAIRS = HEADS // 2
JS = [(hh, qb) for hh in range(2) for qb in range(QB)]


def pe_values(c, pe, cur, V_width):
    for tile in tiles(pe, cur, V_width // 256):
        pe_token_tile(c, pe, tile, c.XH, c.XL)


def pe_token_tile(c, pe, tile, XH, XL, tokens=S):
    pe.wait_ge(c.sem("w_split"), tile.t + 1)
    pe.wait_ge(c.sem("ps_done"), tile.n + 1)
    WH = c.WH[tile.p][:, :].rearrange("p (k c) -> p k c", k=DC)
    WL = c.WL[tile.p][:, :].rearrange("p (k c) -> p k c", k=DC)
    for tb in range(tokens // P):
        out = c.PB[:, tile.b + tb // 2, (tb % 2) * 256:(tb % 2) * 256 + 256]
        for k in range(DC):
            last = mm3(c, out, XH[:, k, tb * P:tb * P + P], XL[:, k, tb * P:tb * P + P], WH[:, k, :], WL[:, k, :],
                       k == 0, k == DC - 1)
    last.then_inc(c.sem("tile_done"), 1)


def act_values(c, act, cur, V, width, tokens=S):
    for tile in tiles(act, cur, width // 256):
        act_next(c, act, tile)
        act.wait_ge(c.sem("tile_done"), tile.t + 3)
        for tb in range(0, tokens // P, 2):
            src = c.PB[:, tile.b + tb // 2, :].rearrange("p (t c) -> p t c", t=2)
            last = c.nc.scalar.activation(V[:, tb:tb + 2, bass.ds(tile.k * 256, 256)], src, ACT.Copy)
        last.then_inc(c.sem("ps_done"), 1)


def dve_values(c, dve, cur, width):
    for tile in tiles(dve, cur, width // 256):
        dve_next(c, dve, tile)


def pe_forget(c, pe, cur):
    for tile in tiles(pe, cur, 1, 2):
        pe.wait_ge(c.sem("w_split"), tile.t + 1)
        pe.wait_ge(c.sem("ps_done"), tile.n + 1)
        WH = c.WH[tile.p][:, :DC * P].rearrange("p (k c) -> p k c", k=DC)
        WL = c.WL[tile.p][:, :DC * P].rearrange("p (k c) -> p k c", k=DC)
        for k in range(DC):
            last = mm3(c, c.PB[:, tile.b, :], WH[:, k, :], WL[:, k, :], c.XH[:, k, :], c.XL[:, k, :],
                       k == 0, k == DC - 1)
        last.then_inc(c.sem("tile_done"), 1)


def dve_log1p(c, dve, u, z, z2, q):
    dve_log1p_argument(c, dve, u, z, z2)
    dve_log1p_series(c, dve, z, z2, q)


def dve_log1p_argument(c, dve, u, z, z2):
    V = c.nc.vector
    V.tensor_scalar_add(z, u, 2.0)
    dve.drain()
    V.reciprocal(z, z)
    dve.drain()
    V.tensor_tensor(z, z, u, ALU.mult)
    dve.drain()
    V.tensor_tensor(z2, z, z, ALU.mult)
    dve.drain()


def dve_log1p_series(c, dve, z, z2, q):
    V = c.nc.vector
    V.tensor_scalar(q, z2, 1.0 / 17, None, ALU.mult)
    dve.drain()
    for m in (15, 13, 11, 9, 7, 5, 3):
        V.scalar_tensor_tensor(out=q, in0=q, scalar=1.0 / m, in1=z2, op0=ALU.add, op1=ALU.mult)
        dve.drain()
    V.scalar_tensor_tensor(out=q, in0=q, scalar=1.0, in1=z, op0=ALU.add, op1=ALU.mult)
    dve.drain()


def act_forget(c, act, cur, l):
    for tile in tiles(act, cur, 1, 2):
        act_next(c, act, tile)
        act.wait_ge(c.sem("f_abs"), l + 1)
        c.nc.scalar.activation(c.FW[:, 1, :], c.FW[:, 1, :], ACT.Exp, scale=-1.0).then_inc(c.sem("f_exp"), 1)


def dve_forget(c, dve, cur, l):
    V = c.nc.vector
    F = c.FW
    for tile in tiles(dve, cur, 1, 2):
        dve_next(c, dve, tile)
        dve.wait_ge(c.sem("tile_done"), tile.t + 3)
        col = PRM["b_f"][0]
        V.tensor_scalar(F[:, 0, :], c.PB[:, tile.b, :], c.PR[:, l, col:col + 1], None, ALU.add)\
            .then_inc(c.sem("ps_done"), 2)
        dve.drain()
        V.tensor_scalar(F[:, 1, :], F[:, 0, :], -1.0, None, ALU.mult)
        dve.drain()
        V.tensor_tensor(F[:, 1, :], F[:, 1, :], F[:, 0, :], ALU.max).then_inc(c.sem("f_abs"), 1)
        V.tensor_scalar_min(F[:, 0, :], F[:, 0, :], 0.0)
        dve.wait_ge(c.sem("f_exp"), l + 1)
        dve_log1p_argument(c, dve, F[:, 1, :], F[:, 2, :], F[:, 3, :])
    dve_next(c, dve, one_tile(cur))
    dve_log1p_series(c, dve, F[:, 2, :], F[:, 3, :], F[:, 4, :])
    dve_next(c, dve, one_tile(cur))
    V.scalar_tensor_tensor(out=F[:, 0, :], in0=F[:, 4, :], scalar=-2.0, in1=F[:, 0, :], op0=ALU.mult, op1=ALU.add)
    V.memset(F[:, 2, :], 1.0)
    V.memset(c.CQ[:, :], 1.0)
    V.memset(c.KZ[0][:, :], 1.0)
    V.memset(c.KZ[1][:, :], 1.0)
    dve.drain()
    V.tensor_tensor_scan(F[:, 1, :], F[:, 2, :], F[:, 0, :], 0.0, ALU.mult, ALU.add)
    dve.drain()
    for r in (32, 96):
        V.tensor_copy(c.CQ[r:r + 32, :], F[r:r + 32, 1, :])
    V.tensor_scalar(c.KZ[1][0:32, :], F[0:32, 1, :], -1.0, None, ALU.mult)
    V.tensor_scalar(c.KZ[0][64:96, :], F[64:96, 1, :], -1.0, None, ALU.mult)
    dve.drain()


def pe_attention(c, pe, cur, l):
    pe_forget(c, pe, cur)
    pe_values(c, pe, cur, D)
    def head_sums(i, b):
        pe.wait_ge(c.sem("qk_sq"), l * PAIRS + i + 1)
        for g in range(2):
            last = c.nc.tensor.matmul(c.PB[:, 6 + g, :], c.ONESB[:, :], c.SQ2[:, g, :], start=True, stop=True)
        last.then_inc(c.sem("qk_sum"), 1)

    def attend(i, b, n):
        pe.wait_ge(c.sem("qk_ready"), l * PAIRS + i + 1)
        def step(hh, qb):
            def scores(S):
                nk = P * qb + P
                c.nc.tensor.matmul(S[:, :nk], c.QZ[hh][:, qb * P:qb * P + P], c.KZ[hh][:, :nk],
                                   start=True, stop=False)
                return c.nc.tensor.matmul(S[:, nk - P:nk], c.IDENT[:, :], c.CAUSAL[:, :], start=False, stop=True)
            return {"nk": P * qb + P, "scores": scores,
                    "values": lambda kb: c.V[:, kb, bass.ds(i * P + hh * HD, HD)],
                    "out": c.PB[:, b, qb * P + hh * HD:qb * P + hh * HD + HD]}
        pe_steps(c, pe, Steps((l * PAIRS + i) * 8, [step(*x) for x in JS], (c.PM, c.PT, c.SUM)))

    def turn(i, b):
        pe.wait_ge(c.sem("o_ready"), l * PAIRS + i + 1)
        for qb in range(QB):
            last = c.nc.tensor.transpose(c.PB[:, b + 1, qb * P:qb * P + P], c.OQ[:, qb, :], c.IDENT[:, :])
        last.then_inc(c.sem("ot_ready"), 1)

    def gate_tile():
        pe_pair_tile(c, pe, Tile(cur, 0, PAIRS, 1), c.XH, c.XL)
    pair_schedule(c, pe, cur, "pe", head_sums, attend, turn, last_work=gate_tile)
    phase_end(c, pe, cur)


def pair_schedule(c, eng, cur, kind, norm, attend, outputs, tile_work=None, last_work=None):
    def project(tile):
        if kind == "pe":
            pe_pair_tile(c, eng, tile, c.XH, c.XL)
        elif kind == "act":
            act_next(c, eng, tile)
        else:
            dve_next(c, eng, tile)
        if tile_work:
            tile_work(tile)

    def step(i, before, tile):
        project(tile)
        attend(i, before.b, before.n)
        outputs(i, before.b)
        norm(i + 1, tile.b)
    first = Tile(cur, 0, 0, 1)
    project(first)
    norm(0, first.b)
    with eng.Fori(0, PAIRS // 2 - 1) as i:
        for j in (1, 2):
            step(i * 2 + (j - 1), Tile(cur, i, j - 1, 1), Tile(cur, i, j, 1))
    tile, before = Tile(cur, 0, PAIRS - 1, 1), Tile(cur, 0, PAIRS - 2, 1)
    step(PAIRS - 2, before, tile)
    if last_work:
        last_work()
    attend(PAIRS - 1, tile.b, tile.n)
    outputs(PAIRS - 1, tile.b)
    cur.t += PAIRS
    cur.n += PAIRS


def act_attention(c, act, cur, l):
    act_forget(c, act, cur, l)
    act_values(c, act, cur, c.V, D)
    base = l * PAIRS

    def squares(tile):
        act.wait_ge(c.sem("tile_done"), tile.t + 3)
        c.nc.scalar.activation(c.SQ2[:, :, :], c.PB[:, tile.b:tile.b + 2, :], ACT.Square).then_inc(c.sem("qk_sq"), 1)

    def roots(i, b):
        act.wait_ge(c.sem("qk_sum"), base + i + 1)
        c.nc.scalar.activation(c.RS2[:, :, :], c.PB[:, 6:8, :], ACT.Sqrt, bias=c.EPSC[:, 0:1], scale=1.0 / HD)\
            .then_inc(c.sem("qk_root"), 1)

    def attend(i, b, n):
        act_steps(c, act, Steps((base + i) * 8, [{"nk": P * qb + P} for hh, qb in JS], (c.PM, c.PT, c.SUM),
                                [qb * 2 + hh for hh, qb in JS]))

    def outputs(i, b):
        act.wait_ge(c.sem("ot_ready"), base + i + 1)
        c.nc.scalar.activation(c.YH[:, i, :], c.PB[:, b + 1, :], ACT.Copy).then_inc(c.sem("ot_hi"), 1)

    pair_schedule(c, act, cur, "act", roots, attend, outputs, squares)
    phase_end(c, act, cur)


def dve_attention(c, dve, cur, l):
    V = c.nc.vector
    dve_forget(c, dve, cur, l)
    for _ in range(2):
        dve_next(c, dve, one_tile(cur))
    base = l * PAIRS

    def norm(i, b):
        dve.wait_ge(c.sem("qk_root"), base + i + 1)
        V.reciprocal(c.RS2[:, :, :], c.RS2[:, :, :])
        dve.drain()
        for hh in range(2):
            own, other = slice(hh * HD, hh * HD + HD), slice(HD - hh * HD, P - hh * HD)
            V.scalar_tensor_tensor(out=c.QZ[hh][own, :], in0=c.PB[own, b, :], scalar=c.GQ8[own, l, 0:1],
                                   in1=c.RS2[own, 0, :], op0=ALU.mult, op1=ALU.mult)
            col = PRM["g_k"][0]
            V.scalar_tensor_tensor(out=c.KZ[hh][own, :], in0=c.PB[own, b + 1, :], scalar=c.PR[own, l, col:col + 1],
                                   in1=c.RS2[own, 1, :], op0=ALU.mult, op1=ALU.mult)
            last = V.tensor_scalar(c.QZ[hh][other, :], c.CQ[other, :], c.HMASK[other, bass.ds(i * 2 + hh, 1)], None,
                                   ALU.mult)
        last.then_inc(c.sem("qk_ready"), 1)

    def attend(i, b, n):
        dve_steps(c, dve, Steps((base + i) * 8, [{"nk": P * qb + P} for hh, qb in JS], (c.PM, c.PT, c.SUM)))
        V.reciprocal(c.SUM[:, 0:8], c.SUM[:, 0:8])
        dve.drain()
        dve.wait_ge(c.sem("pv_done"), (base + i) * 8 + 10)
        V.tensor_tensor(c.OQ[:, :, :].rearrange("p q (h d) -> p (q h) d", h=2),
                        c.PB[:, b, :].rearrange("p (e d) -> p e d", d=HD),
                        c.SUM[:, 0:8].unsqueeze(2).to_broadcast([P, 8, HD]), ALU.mult).then_inc(c.sem("o_ready"), 1)

    def outputs(i, b):
        dve.wait_ge(c.sem("ot_hi"), base + i + 1)
        V.tensor_tensor(c.YL[:, i, :], c.PB[:, b + 1, :], c.YH[:, i, :].bitcast(F32), ALU.subtract)\
            .then_inc(c.sem("ps_done"), 1)

    pair_schedule(c, dve, cur, "dve", norm, attend, outputs)
    phase_end(c, dve, cur)




CONSTS = {}
for _n, _w in (("ident", 128), ("ones", 128), ("ones_head", 128), ("causal", 128), ("head_mask", 16)):
    CONSTS[_n] = (sum(w for _, w in CONSTS.values()), _w)
NCONST = sum(w for _, w in CONSTS.values())


def constants():
    t = np.zeros((P, NCONST), np.float32)

    def put(name, a):
        at, w = CONSTS[name]
        t[:, at:at + w] = a
    i = np.arange(P)
    put("ident", np.eye(P))
    put("ones", 1.0)
    put("ones_head", (i[:, None] // HD == i[None, :] // HD))
    put("causal", np.where(i[None, :] <= i[:, None], 0.0, NEG))
    put("head_mask", (i[:, None] % 32 == np.arange(16)[None, :]))
    return t


def allocate(c):
    c.PB = c.stack.enter_context(c.nc.psum_tensor("PB", [P, 8, S], F32))
    c.X = c.sb("X", [P, DC, S])
    c.XH, c.XL = c.sb("XH", [P, DC, S], F32R), c.sb("XL", [P, DC, S], F32R)
    c.RAW = [c.sb(f"RAW{i}", [P, TILE]) for i in range(2)]
    c.WH = [c.sb(f"WH{i}", [P, TILE], F32R) for i in range(2)]
    c.WL = [c.sb(f"WL{i}", [P, TILE], F32R) for i in range(2)]
    c.PR = c.sb("PR", [P, LAYERS, NPRM])
    c.CT = c.sb("CT", [P, NCONST])
    c.IDENT, c.ONES, c.ONESB, c.CAUSAL, c.HMASK = (
        c.CT[:, CONSTS[n][0]:sum(CONSTS[n])] for n in ("ident", "ones", "ones_head", "causal", "head_mask"))
    c.EPSC = c.sb("EPSC", [P, 1])
    c.SPN2 = c.sb("SPN2", [P, LAYERS, DC])
    c.SPP, c.SPN = c.sb("SPP", [P, LAYERS, DC]), c.sb("SPN", [P, LAYERS, DC])
    c.GQ8 = c.sb("GQ8", [P, LAYERS, 1])
    allocate2(c)
    c.NM, c.SUM = c.sb("NM", [P, 2]), c.sb("SUM", [P, 8])

    with ExitStack() as s:
        c.SQ = c.sb("SQ", [P, DC, S], F32, s)
        c.RS = c.sb("RS", [P, S], F32, s)
        c.LW = c.sb("LW", [P, 6, LAYERS, DC], F32, s)
    with ExitStack() as s:
        c.HH, c.HL = c.sb("HH", [P, FC, S], F32R, s), c.sb("HL", [P, FC, S], F32R, s)
        c.SIL, c.PROD = c.sb("SIL", [P, 2, S], F32, s), c.sb("PROD", [P, 2, S], F32, s)
    with ExitStack() as y:
        c.YH, c.YL = c.sb("YH", [P, DC, S], F32R, y), c.sb("YL", [P, DC, S], F32R, y)
        with ExitStack() as s:
            c.ZX, c.XR, c.LG, c.AA = (c.sb(n, [P, DC, S], F32, s) for n in ("ZX", "XR", "LG", "AA"))
            c.SG = c.sb("SG", [P, 4, S], F32, s)
        c.M = c.sb("M", [P, DC, S], F32, y)
        with ExitStack() as s:
            c.SG2 = c.sb("SG2", [P, 4, S], F32, s)
            c.MH, c.ML = c.sb("MH", [P, DC, S], F32R, s), c.sb("ML", [P, DC, S], F32R, s)
        with ExitStack() as s:
            c.V = c.sb("V", [P, QB, D], F32, s)
            c.FW = c.sb("FW", [P, 5, S], F32, s)
            c.CQ = c.sb("CQ", [P, S], F32, s)
            c.KZ = [c.sb(f"KZ{i}", [P, S], F32, s) for i in range(2)]
            c.QZ = [c.sb(f"QZ{i}", [P, S], F32, s) for i in range(2)]
            c.SQ2, c.RS2 = c.sb("SQ2", [P, 2, S], F32, s), c.sb("RS2", [P, 2, S], F32, s)
            c.PM, c.PT = c.sb("PM", [P, 2, S], F32, s), c.sb("PT", [P, 2, S], F32, s)
            c.OQ = c.sb("OQ", [P, QB, P], F32, s)
    allocate2_arena(c)



def sp_setup(c, sp, d):
    sp.dma_start(c.X[:, :, :], d["x"]).then_inc(c.sem("x_loaded"), 16)
    sp.dma_start(c.CT[:, :], d["consts"]).then_inc(c.sem("tables_loaded"), 16)
    sp.dma_start(c.PR[:, :, :], d["params"]).then_inc(c.sem("params_loaded"), 16)
    sp.dma_start(c.PR2[:, :], d["params2"]).then_inc(c.sem("params2_loaded"), 16)
    sp.dma_start(c.CT2[:, :], d["consts2"]).then_inc(c.sem("tables2_loaded"), 16)


def pe_setup(c, pe):
    for name in ("tile_done", "ps_done", "p_ready", "pt_copied", "pv_done", "pt_ready", "gm_full", "gm_copied",
                 "y_added", "picked",
                 "top_done"):
        pe.sem_inc(c.sem(name), 2)
    for name in ("nsa_out", "ps_scores", "key_scores", "y_done"):
        pe.sem_inc(c.sem(name), 1)
    for s in range(2):
        pe.sem_inc(c.sem(f"gm_stored{s}"), 16)
    pe.wait_ge(c.sem("tables_loaded"), 16)
    pe.wait_ge(c.sem("tables2_loaded"), 16)
    pe.wait_ge(c.sem("params2_loaded"), 16)


def prm(c, name):
    at, w = PRM[name]
    return c.PR[:, :, at:at + w]


def act_setup(c, act):
    act.wait_ge(c.sem("lam_abs"), 1)
    c.nc.scalar.activation(c.LW[:, 1], c.LW[:, 1], ACT.Exp, scale=-1.0).then_inc(c.sem("lam_exp"), 1)
    act.wait_ge(c.sem("setup_done"), 1)
    act.wait_ge(c.sem("x_loaded"), 16)


def dve_setup(c, dve):
    V = c.nc.vector
    V.memset(c.EPSC[:, :], EPS)
    dve.wait_ge(c.sem("params_loaded"), 16)
    dve.wait_ge(c.sem("tables_loaded"), 16)
    dve.wait_ge(c.sem("tables2_loaded"), 16)
    dve.wait_ge(c.sem("params2_loaded"), 16)
    V.tensor_scalar(c.GQ8[:, :, :], prm(c, "g_q"), HD ** -0.5, None, ALU.mult)
    L = c.LW
    V.tensor_scalar(L[:, 0], prm(c, "lam"), -1.0, None, ALU.mult)
    dve.drain()
    V.tensor_tensor(L[:, 1], L[:, 0], prm(c, "lam"), ALU.max).then_inc(c.sem("lam_abs"), 1)
    V.tensor_scalar_max(L[:, 0], L[:, 0], 0.0)
    dve.wait_ge(c.sem("lam_exp"), 1)
    dve_log1p(c, dve, L[:, 1], L[:, 2], L[:, 3], L[:, 4])
    V.scalar_tensor_tensor(out=L[:, 0], in0=L[:, 4], scalar=2.0, in1=L[:, 0], op0=ALU.mult, op1=ALU.add)
    dve.drain()
    V.tensor_scalar(c.SPP[:, :, :], L[:, 0], 8.0, None, ALU.mult)
    V.tensor_scalar(c.SPN[:, :, :], L[:, 0], -8.0, None, ALU.mult)
    V.tensor_scalar(c.SPN2[:, :, :], L[:, 0], -16.0, None, ALU.mult)
    dve.drain().then_inc(c.sem("setup_done"), 1)
    dve.wait_ge(c.sem("x_loaded"), 16)
    dve.sem_inc(c.sem("x_new"), 4)



def pe_layer(c, pe, cur, l):
    pe_norm(c, pe, l * 3, bank=0)
    pe_ffn(c, pe, cur, l * 2, l * 3)
    pe_norm(c, pe, l * 3 + 1, bank=0)
    pe_lru(c, pe, cur, l)
    pe_attention(c, pe, cur, l)
    pe_gated(c, pe, cur)
    pe_residual(c, pe, cur, c.MH, c.ML, False)
    pe_norm(c, pe, l * 3 + 2)
    pe_ffn(c, pe, cur, l * 2 + 1, l * 3 + 2)


def act_layer(c, act, cur, l):
    act_norm(c, act, l * 3, c.X, c.XH, bank=0, news=l * 12)
    act_ffn(c, act, cur, l * 2)
    act_norm(c, act, l * 3 + 1, c.X, c.XH, bank=0, news=l * 12 + 4)
    act_lru(c, act, cur, l)
    act_attention(c, act, cur, l)
    act_gated(c, act, cur, l)
    act_residual(c, act, cur, False)
    act_norm(c, act, l * 3 + 2, c.X, c.XH, news=l * 12 + 8)
    act_ffn(c, act, cur, l * 2 + 1)


def dve_layer(c, dve, cur, l):
    def gain(name):
        at = PRM[name][0]
        return lambda k: c.PR[:, l, at + k:at + k + 1]
    dve_norm(c, dve, l * 3, c.X, gain("g_ffn1"), c.XH, c.XL)
    dve_ffn(c, dve, cur, l * 2)
    dve_norm(c, dve, l * 3 + 1, c.X, gain("g_mix"), c.XH, c.XL)
    dve_lru(c, dve, cur, l)
    dve_attention(c, dve, cur, l)
    dve_gated(c, dve, cur, l)
    dve_residual(c, dve, cur, False)
    dve_norm(c, dve, l * 3 + 2, c.X, gain("g_ffn2"), c.XH, c.XL)
    dve_ffn(c, dve, cur, l * 2 + 1)




CONV_K = 31
CC = 4
N_CMP = (S - 32) // 16 + 1
N_WIN = 34
KV_PAD = 33 * 16 + 32
MEM = 256
MEM_H = 4
MHD = D // MEM_H
KEYS = 128
TOPK = 16
PH = 8
N_EXP = KEYS
TOK_BLOCK = 64

BLOCK2_TILES = (("ab", 4), ("q", 2), ("cv", 1), ("ks", 1), ("kw", 1), ("vsw", 1), ("gates", 1), ("cmp", 4),
                ("w_out", 4), ("mem_k", 4), ("mem_v", 4), ("mem_q", 4), ("mem_o", 4), ("peer_q", 8))
T_PEER = LAYERS * TL + sum(n for _, n in BLOCK2_TILES)
NT = T_PEER + N_EXP

PRM2 = {}
for _n, _w in (("mix_g", 8), ("dw_w", CC * CONV_K), ("dw_b", CC), ("ln_g", CC), ("ln_b", CC), ("cmp_b1", 2),
               ("cmp_b2k", 1), ("cmp_b2v", HD), ("cmp_pos", 64), ("cmp_w2k", P), ("cmp_w2v", HD), ("memq_g", 8),
               ("memkv_g", 8), ("peer_g", 8), ("final_g", 8)):
    PRM2[_n] = (sum(w for _, w in PRM2.values()), _w)
NPRM2 = sum(w for _, w in PRM2.values())
CONSTS2 = {}
for _n, _w in (("rot", P), ("inv", 1), ("cmask", QB * 32), ("row_ok", 1), ("iota", P)):
    CONSTS2[_n] = (sum(w for _, w in CONSTS2.values()), _w)
NCONST2 = sum(w for _, w in CONSTS2.values())


def constants2():
    t = np.zeros((P, NCONST2), np.float32)

    def put(name, a):
        at, w = CONSTS2[name]
        t[:, at:at + w] = a
    rot_dim = HD // 4
    half = rot_dim // 2
    rot = np.zeros((P, P), np.float32)
    inv = np.zeros((P, 1), np.float32)
    freq = np.float32(500000.0) ** (-(np.arange(half, dtype=np.float32) * np.float32(2.0) / np.float32(rot_dim)))
    for h in (0, HD):
        for i in range(half):
            rot[h + i + half, h + i] = -1.0
            rot[h + i, h + i + half] = 1.0
            inv[h + i, 0] = inv[h + i + half, 0] = freq[i]
    put("rot", rot)
    put("inv", inv)
    tok = np.arange(P)[:, None, None] + P * np.arange(QB)[None, :, None]
    ok = np.arange(32)[None, None, :] * 16 + 31 <= tok
    put("cmask", np.where(ok, 0.0, NEG).reshape(P, -1))
    put("row_ok", (np.arange(P) >= 31)[:, None])
    put("iota", np.arange(P)[None, :])
    return t


def p2(c, name, a=0, n=None):
    at, w = PRM2[name]
    return c.PR2[:, at + a:at + (w if n is None else a + n)]


def c2(c, name):
    at, w = CONSTS2[name]
    return c.CT2[:, at:at + w]


def allocate2(c):
    c.PR2 = c.sb("PR2", [P, NPRM2])
    c.CT2 = c.sb("CT2", [P, NCONST2])


def allocate2_arena(c):
    with ExitStack() as s:
        c.YH2, c.YL2 = c.sb("YH2", [P, DC, S], F32R, s), c.sb("YL2", [P, DC, S], F32R, s)
        with ExitStack() as q:
            c.UC = c.sb("UC", [P, CC, S + CONV_K - 1], F32, q)
            c.YC = c.sb("YC", [P, CC, S], F32, q)
            c.QRAW = c.sb("QRAW", [P, CC, S], F32, q)
            c.KCH, c.KCL = c.sb("KCH", [P, 2, KV_PAD], F32R, q), c.sb("KCL", [P, 2, KV_PAD], F32R, q)
            c.KS, c.KW = c.sb("KS", [P, 2, S], F32, q), c.sb("KW", [P, 2, S], F32, q)
            c.VSW = c.sb("VSW", [P, QB, 256], F32, q)
            c.GT = c.sb("GT", [P, QB, 24], F32, q)
            c.COS, c.SIN = c.sb("COS", [P, S], F32, q), c.sb("SIN", [P, S], F32, q)
            c.HT, c.BC = c.sb("HT", [P, 2, 2, P], F32, q), c.sb("BC", [P, 2, 2], F32, q)
            c.HDN = c.sb("HDN", [P, 2, 2, 32], F32, q)
            c.KC, c.VC = c.sb("KC", [P, 2, 32], F32, q), c.sb("VC", [P, 2, HD], F32, q)
            with ExitStack() as r:
                c.T2 = c.sb("T2", [P, 4, S], F32, r)
                c.SGB = c.sb("SGB", [P, 2, S], F32, r)
                c.KVC = c.sb("KVC", [P, 2, KV_PAD], F32, r)
            with ExitStack() as r:
                c.QZR = [c.sb(f"QZR{i}", [P, S], F32, r) for i in range(2)]
                c.QZC = [c.sb(f"QZC{i}", [P, S], F32, r) for i in range(2)]
                c.PM2, c.PT2 = c.sb("PM2", [P, 2, S], F32, r), c.sb("PT2", [P, 2, S], F32, r)
                c.OQ2, c.OB2 = c.sb("OQ2", [P, QB, P], F32, r), c.sb("OB2", [P, QB, P], F32, r)
                c.SUM2 = c.sb("SUM2", [P, 3, 8], F32, r)
        with ExitStack() as q:
            c.MEMX = c.sb("MEMX", [P, DC, MEM], F32, q)
            c.MK = c.sb("MK", [P, DC, MEM], F32, q)
            c.MV = c.sb("MV", [P, MEM // P, D], F32, q)
            c.MQ = c.sb("MQ", [P, DC, S], F32, q)
            c.MQS = c.sb("MQS", [P, 2, S], F32, q)
            c.PM3, c.PT3 = c.sb("PM3", [P, 2, S], F32, q), c.sb("PT3", [P, 2, S], F32, q)
            c.OQ3 = c.sb("OQ3", [P, QB, MHD], F32, q)
            c.SUM3 = c.sb("SUM3", [P, QB], F32, q)
    with ExitStack() as s:
        c.RI1, c.RI2, c.RGT = (c.sb(n, [P, QB, P], F32, s) for n in ("RI1", "RI2", "RGT"))
        c.IT1, c.IT2, c.GTT = (c.sb(n, [P, S + 8], F32, s) for n in ("IT1", "IT2", "GTT"))
        with ExitStack() as q:
            c.SK = c.sb("SK", [P, 2 * PH, KEYS], F32, q)
            c.QP = c.sb("QP", [P, 2, S], F32, q)
            c.SC = [c.sb(f"SC{i}", [P, 2, QB, KEYS], F32, q) for i in range(2)]
            c.SC2 = c.sb("SC2", [P, 1024], F32, q)
            c.TV = c.sb("TV", [P, 2, QB, TOPK], F32, q)
            c.TI = c.sb("TI", [P, 2, QB, TOPK], U32, q)
            c.TF = [c.sb(f"TF{i}", [P, 2, QB, TOPK], F32, q) for i in range(2)]
            c.CAND = c.sb("CAND", [P, QB, 256], F32, q)
            c.BV = c.sb("BV", [P, QB, TOPK], F32, q)
            c.BI = c.sb("BI", [P, 3, QB, TOPK], U32, q)
            c.BF = [c.sb(f"BF{i}", [P, 2, QB, TOPK], F32, q) for i in range(2)]
            c.EQ = c.sb("EQ", [P, QB, TOPK, TOPK], F32, q)
            c.GS = c.sb("GS", [P, 2, QB * PH], F32, q)
        with ExitStack() as q:
            c.OA = [c.sb(f"OA{i}", [P, 4, P], F32, q) for i in range(2)]
            c.OB = [c.sb(f"OB{i}", [P, 4, P], F32, q) for i in range(2)]
            c.HS = [c.sb(f"HS{i}", [P, P], F32, q) for i in range(2)]
            c.HP = [c.sb(f"HP{i}", [P, P], F32, q) for i in range(2)]
            c.STG = [c.sb(f"STG{i}", [P, KEYS, TOK_BLOCK], F32, q) for i in range(2)]
    with ExitStack() as s:
        c.AG, c.WG = c.sb("AG", [P, 2, S], F32, s), c.sb("WG", [P, 2, S], F32, s)
        c.WGH, c.WGL = c.sb("WGH", [P, 2, S], F32R, s), c.sb("WGL", [P, 2, S], F32R, s)
        c.GM = [c.sb(f"GM{i}", [P, S], F32, s) for i in range(4)]
        c.YACC = c.sb("YACC", [P, 4, S], F32, s)
    with ExitStack() as s:
        c.FIN_SQ = c.sb("FIN_SQ", [P, DC + 1, S], F32, s)
        c.FIN = c.sb("FIN", [P, DC, S], F32, s)



def pe_gate_tile(c, pe, tile):
    pe.wait_ge(c.sem("w_split"), tile.t + 1)
    pe.wait_ge(c.sem("ps_done"), tile.n + 1)
    WH = c.WH[tile.p][:, :DC * 24].rearrange("p (k c) -> p k c", k=DC)
    WL = c.WL[tile.p][:, :DC * 24].rearrange("p (k c) -> p k c", k=DC)
    for tb in range(QB):
        for k in range(DC):
            last = mm3(c, c.PB[:, tile.b, tb * 24:tb * 24 + 24], c.XH[:, k, tb * P:tb * P + P],
                       c.XL[:, k, tb * P:tb * P + P], WH[:, k, :], WL[:, k, :], k == 0, k == DC - 1)
    last.then_inc(c.sem("tile_done"), 1)


def pe_proj2(c, pe, cur):
    pe_normed_tile(c, pe, cur, V2)
    for tile in tiles(pe, cur, 3):
        pe_pair_tile(c, pe, tile, c.XH, c.XL)
    for tile in tiles(pe, cur, 2):
        pe_pair_tile(c, pe, tile, c.XH, c.XL)
    for what in ("cv", "ks", "kw"):
        pe_pair_tile(c, pe, one_tile(cur), c.XH, c.XL)

    def rotate(n):
        pe.wait_ge(c.sem("k_raw"), n + 1)
        if n:
            pe.wait_ge(c.sem("k_done"), n)
        for g in range(2):
            last = c.nc.tensor.matmul(c.PB[:, 6 + g, :], c2(c, "rot"), c.T2[:, 2 * n + g, :],
                                      start=True, stop=True)
        last.then_inc(c.sem("k_rot"), 1)
    rotate(0)
    pe_token_tile(c, pe, one_tile(cur), c.XH, c.XL)
    pe_gate_tile(c, pe, one_tile(cur))
    pe.wait_ge(c.sem("cmp_in"), 1)
    for kv in range(2):
        for half in range(2):
            tile = Tile(cur, 0, 0, 1)
            b = 2 * ((cur.n + kv) % 2)
            pe.wait_ge(c.sem("w_split"), tile.t + 1)
            if half == 0:
                pe.wait_ge(c.sem("ps_done"), cur.base_n + cur.n + kv + 1)
            WH = c.WH[tile.p][:, :].rearrange("p (r c) -> p r c", r=16)
            WL = c.WL[tile.p][:, :].rearrange("p (r c) -> p r c", r=16)
            for g in range(2):
                rows = slice(g * HD, g * HD + HD)
                for r in range(16):
                    win = slice(half * 16 + r, half * 16 + r + 16 * (N_WIN - 1) + 1, 16)
                    last = mm3(c, c.PB[:N_WIN, b + g, :P], c.KCH[rows, kv, win], c.KCL[rows, kv, win],
                               WH[rows, r, :], WL[rows, r, :], half == 0 and r == 0, half == 1 and r == 15)
            last.then_inc(c.sem("tile_done"), 1)
            cur.t += 1
            if (kv, half) == (0, 0):
                rotate(1)
    cur.n += 2

    def ln_sum(n):
        pe.wait_ge(c.sem("ln_in"), n + 1)
        src = (c.YC, c.T2)[n]
        for k in range(CC):
            last = c.nc.tensor.matmul(c.PB[:, 4, :], c.ONES[:, :], src[:, k, :], start=k == 0, stop=k == CC - 1)
        last.then_inc(c.sem("ln_sum"), 1)
    ln_sum(0)
    pe.wait_ge(c.sem("cmp_raw"), 2)
    pe.wait_ge(c.sem("k_done"), 2)
    for kv in range(2):
        for g in range(2):
            last = c.nc.tensor.transpose(c.PB[:, 6, (kv * 2 + g) * P:(kv * 2 + g) * P + N_WIN],
                                         c.HT[:N_WIN, kv, g, :], c.IDENT[:N_WIN, :N_WIN])
    last.then_inc(c.sem("cmp_turned"), 1)
    pe.wait_ge(c.sem("cmp_hidden"), 2)
    c.nc.tensor.matmul(c.PB[:, 7, :64], p2(c, "cmp_w2k"), c.HDN[:, 0, :, :].rearrange("p g c -> p (g c)"),
                       start=True, stop=True)
    for g in range(2):
        last = c.nc.tensor.matmul(c.PB[:N_CMP, 7, P + g * HD:P + g * HD + HD], c.HDN[:, 1, g, :N_CMP], p2(c, "cmp_w2v"),
                                  start=True, stop=True)
    last.then_inc(c.sem("cmp_out"), 1)
    ln_sum(1)
    phase_end(c, pe, cur)


def act_proj2(c, act, cur):
    A = c.nc.scalar
    act.wait_ge(c.sem("angles"), 1)
    A.activation(c.SIN[:, :], c.SIN[:, :], ACT.Sin)
    A.activation(c.COS[:, :], c.COS[:, :], ACT.Sin).then_inc(c.sem("rope_ready"), 1)
    for tile in tiles(act, cur, 4):
        act_next(c, act, tile)
        act.wait_ge(c.sem("tile_done"), tile.t + 3)
        act.wait_ge(c.sem("ps_done"), tile.n + 1)
        A.activation(c.SGB[:, tile.b // 2, :], c.PB[:, tile.b + 1, :], ACT.Sigmoid).then_inc(c.sem("sig_b"), 1)
    for tile in tiles(act, cur, 2):
        act_next(c, act, tile)
        act.wait_ge(c.sem("tile_done"), tile.t + 3)
        act.wait_ge(c.sem("ps_done"), tile.n + 2)
        A.activation(c.QRAW[:, tile.k * 2:tile.k * 2 + 2, :], c.PB[:, tile.b:tile.b + 2, :], ACT.Copy,
                     scale=HD ** -0.5).then_inc(c.sem("ps_done"), 1)
    for tile in tiles(act, cur, 1):
        act_next(c, act, tile)
        act.wait_ge(c.sem("tile_done"), tile.t + 3)
        A.activation(c.KVC[:, :, :S], c.PB[:, tile.b:tile.b + 2, :], ACT.Copy).then_inc(c.sem("ps_done"), 1)
        act.drain()
        act.wait_ge(c.sem("kvc_pad"), 1)
        A.activation(c.KCH[:, :, :], c.KVC[:, :, :], ACT.Copy).then_inc(c.sem("cmp_hi"), 1)
    for n in range(2):
        for tile in tiles(act, cur, 1):
            act_next(c, act, tile)
            act.wait_ge(c.sem("tile_done"), tile.t + 3)
            A.activation(c.T2[:, 2 * n:2 * n + 2, :], c.PB[:, tile.b:tile.b + 2, :], ACT.Copy)\
                .then_inc(c.sem("ps_done"), 1)
            act.drain().then_inc(c.sem("k_raw"), 1)
    for tile in tiles(act, cur, 1):
        act_next(c, act, tile)
        act.wait_ge(c.sem("tile_done"), tile.t + 3)
        for tb in (0, 2):
            last = A.activation(c.VSW[:, tb:tb + 2, :], c.PB[:, tile.b + tb // 2, :].rearrange("p (t c) -> p t c", t=2),
                                ACT.Copy)
        last.then_inc(c.sem("ps_done"), 1)
    for tile in tiles(act, cur, 1):
        act_next(c, act, tile)
        act.wait_ge(c.sem("tile_done"), tile.t + 3)
        A.activation(c.GT[:, :, :], c.PB[:, tile.b, :QB * 24].rearrange("p (t c) -> p t c", t=QB), ACT.Sigmoid)\
            .then_inc(c.sem("ps_done"), 1)
    for kv in range(2):
        for half in range(2):
            tile = Tile(cur, 0, 0, 1)
            act_next(c, act, tile)
            cur.t += 1
        act.wait_ge(c.sem("tile_done"), tile.t + 3)
        b = 2 * ((cur.n + kv) % 2)
        A.activation(c.HT[:N_WIN, kv, :, :], c.PB[:N_WIN, b:b + 2, :P], ACT.Copy).then_inc(c.sem("ps_done"), 1)
        act.drain().then_inc(c.sem("cmp_raw"), 1)
    cur.n += 2
    act.wait_ge(c.sem("cmp_bias"), 1)
    for kv in range(2):
        for g in range(2):
            at = (kv * 2 + g) * P
            last = A.activation(c.HDN[:, kv, g, :], c.PB[:, 6, at:at + 32], ACT.Gelu_apprx_tanh,
                                bias=c.BC[:, kv, g:g + 1])
        last.then_inc(c.sem("cmp_hidden"), 1)
    act.wait_ge(c.sem("ln_in"), 2)
    act.wait_ge(c.sem("ln_sum"), 2)
    A.activation(c.SGB[:, 0, :], c.PB[:, 4, :], ACT.Sqrt, bias=c.EPSC[:, 0:1], scale=1.0 / 512).then_inc(c.sem("ln_root"), 1)
    act.wait_ge(c.sem("ln_out"), 1)
    A.activation(c.YC[:, :, :], c.YC[:, :, :], ACT.Silu).then_inc(c.sem("conv_silu"), 1)
    act.drain()
    A.activation(c.YH2[:, 0:CC, :], c.YC[:, :, :], ACT.Copy).then_inc(c.sem("conv2_hi"), 1)
    phase_end(c, act, cur)


TWO_PI = 2 * np.pi
PI2_A = 6.28125
PI2_B = float(np.float32(0.0019350051879882812))
PI2_C = float(np.float32(TWO_PI - PI2_A - PI2_B))
ROUND = 12582912.0


def dve_angles(c, dve):
    V = c.nc.vector
    T = c.T2
    dve.wait_ge(c.sem("pos_loaded"), 16)
    V.tensor_copy(T[:, 0, :], c.SGB[:, 0, :].bitcast(I32))
    dve.drain()
    V.tensor_scalar(T[:, 0, :], T[:, 0, :], c2(c, "inv"), None, ALU.mult)
    dve.drain()
    V.tensor_scalar(T[:, 1, :], T[:, 0, :], 1.0 / TWO_PI, None, ALU.mult)
    dve.drain()
    V.tensor_scalar(T[:, 1, :], T[:, 1, :], ROUND, None, ALU.add)
    dve.drain()
    V.tensor_scalar(T[:, 1, :], T[:, 1, :], -ROUND, None, ALU.add)
    dve.drain()
    for part in (PI2_A, PI2_B, PI2_C):
        V.scalar_tensor_tensor(out=T[:, 0, :], in0=T[:, 1, :], scalar=-part, in1=T[:, 0, :], op0=ALU.mult, op1=ALU.add)
        dve.drain()
    V.tensor_scalar(c.SIN[:, :], T[:, 0, :], 3.1415925, -3.1415925, ALU.min, ALU.max)
    V.tensor_scalar(T[:, 2, :], T[:, 0, :], np.pi / 2, None, ALU.add)
    V.tensor_scalar(T[:, 3, :], T[:, 0, :], np.pi / 2, -TWO_PI, ALU.is_gt, ALU.mult)
    dve.drain()
    V.tensor_tensor(T[:, 2, :], T[:, 2, :], T[:, 3, :], ALU.add)
    dve.drain()
    V.tensor_scalar(c.COS[:, :], T[:, 2, :], 3.1415925, -3.1415925, ALU.min, ALU.max)
    dve.drain().then_inc(c.sem("angles"), 1)


def dve_proj2(c, dve, cur):
    V = c.nc.vector
    dve_angles(c, dve)
    V.memset(c.UC[:, :, 0:CONV_K - 1], 0.0)
    V.memset(c.VC[:, :, :], 0.0)
    V.tensor_copy(c.KVC[:, :, S:S + 32], p2(c, "cmp_pos").rearrange("p (v r) -> p v r", v=2))
    V.memset(c.KVC[:, :, S + 32:], 0.0).then_inc(c.sem("kvc_pad"), 1)
    def taps(k, lo, hi):
        for tap in range(lo, hi):
            for m in range(2):
                w = PRM2["dw_w"][0] + (k + m) * CONV_K + tap
                src = c.UC[:, k + m, tap:tap + S]
                acc = c.PB[:, 4 + m, :]
                if tap == 0:
                    b = PRM2["dw_b"][0] + k + m
                    V.tensor_scalar(acc, src, c.PR2[:, w:w + 1], c.PR2[:, b:b + 1], ALU.mult, ALU.add)
                else:
                    V.scalar_tensor_tensor(out=c.YC[:, k + m, :] if tap == CONV_K - 1 else acc, in0=src,
                                           scalar=c.PR2[:, w:w + 1], in1=acc, op0=ALU.mult, op1=ALU.add)
            dve.drain()
    work = [(k, lo, lo + 5 if lo < 25 else CONV_K) for k in (0, 2) for lo in range(0, 30, 5)]

    def some():
        if work:
            taps(*work.pop(0))
    for k in range(CC):
        tile = one_tile(cur)
        dve_next(c, dve, tile)
        dve.wait_ge(c.sem("sig_b"), k + 1)
        V.tensor_tensor(c.UC[:, k, CONV_K - 1:], c.PB[:, tile.b, :], c.SGB[:, tile.b // 2, :], ALU.mult)\
            .then_inc(c.sem("ps_done"), 1)
        if k >= 2:
            dve.drain()
            some()
    for _ in range(2):
        dve_next(c, dve, one_tile(cur))
        some()
    dve_next(c, dve, one_tile(cur))
    dve.wait_ge(c.sem("cmp_hi"), 1)
    V.tensor_tensor(c.KCL[:, :, :], c.KVC[:, :, :], c.KCH[:, :, :].bitcast(F32), ALU.subtract)\
        .then_inc(c.sem("cmp_in"), 1)
    some()
    dve.wait_ge(c.sem("rope_ready"), 1)

    def rope(n):
        K = (c.KS, c.KW)[n]
        dve.wait_ge(c.sem("k_rot"), n + 1)
        for g in range(2):
            V.tensor_tensor(K[:, g, :], c.PB[:, 6 + g, :], c.SIN[:, :], ALU.mult)
            V.tensor_tensor(c.T2[:, 2 * n + g, :], c.T2[:, 2 * n + g, :], c.COS[:, :], ALU.mult)
        dve.drain()
        V.tensor_tensor(K[:, :, :], K[:, :, :], c.T2[:, 2 * n:2 * n + 2, :], ALU.add).then_inc(c.sem("k_done"), 1)
    for _ in range(2):
        dve_next(c, dve, one_tile(cur))
        some()
    dve_next(c, dve, one_tile(cur))
    rope(0)
    some()
    dve_next(c, dve, one_tile(cur))
    some()
    for k in range(4):
        tile = Tile(cur, 0, 0, 1)
        dve_next(c, dve, tile)
        cur.t += 1
        if k == 1:
            rope(1)
        some()
    cur.n += 2
    assert not work
    dve.drain().then_inc(c.sem("ln_in"), 1)
    dve.wait_ge(c.sem("ln_sum"), 1)
    for k in range(CC):
        V.scalar_tensor_tensor(out=c.YC[:, k, :], in0=c.PB[:, 4, :], scalar=-1.0 / 512, in1=c.YC[:, k, :],
                               op0=ALU.mult, op1=ALU.add)
    dve.drain()
    V.tensor_tensor(c.T2[:, :, :], c.YC[:, :, :], c.YC[:, :, :], ALU.mult).then_inc(c.sem("ln_in"), 1)
    dve.wait_ge(c.sem("cmp_turned"), 1)
    V.tensor_tensor(c.BC[:, :, :], c.PB[:, 6, :].rearrange("p (v g c) -> p v g c", v=2, g=2)[:, :, :, 32],
                    p2(c, "cmp_b1").unsqueeze(2).to_broadcast([P, 2, 2]), ALU.add).then_inc(c.sem("cmp_bias"), 1)
    dve.wait_ge(c.sem("cmp_out"), 1)
    V.tensor_scalar(c.KC[:, :, :], c.PB[:, 7, :64].rearrange("p (g c) -> p g c", g=2), p2(c, "cmp_b2k"), None, ALU.add)
    for g in range(2):
        V.tensor_tensor(c.VC[:N_CMP, g, :], c.PB[:N_CMP, 7, P + g * HD:P + g * HD + HD], p2(c, "cmp_b2v")[:N_CMP, :],
                        ALU.add)
    dve.wait_ge(c.sem("ln_root"), 1)
    V.reciprocal(c.SGB[:, 0, :], c.SGB[:, 0, :])
    dve.drain()
    for k in range(CC):
        g = PRM2["ln_g"][0] + k
        V.scalar_tensor_tensor(out=c.YC[:, k, :], in0=c.YC[:, k, :], scalar=c.PR2[:, g:g + 1], in1=c.SGB[:, 0, :],
                               op0=ALU.mult, op1=ALU.mult)
    dve.drain()
    for k in range(CC):
        b = PRM2["ln_b"][0] + k
        last = V.tensor_scalar(c.YC[:, k, :], c.YC[:, k, :], c.PR2[:, b:b + 1], None, ALU.add)
    last.then_inc(c.sem("ln_out"), 1)
    dve.wait_ge(c.sem("conv2_hi"), 1)
    V.tensor_tensor(c.YL2[:, 0:CC, :], c.YC[:, :, :], c.YH2[:, 0:CC, :].bitcast(F32), ALU.subtract)
    phase_end(c, dve, cur)


BRANCH_STEPS = [(br, hh, qb) for br in range(3) for hh in range(2) for qb in range(QB)]
STEPS_LAYERS = LAYERS * PAIRS * 8


def nsa_nk(br, qb):
    return 32 if br == 0 else P * qb + P


def nsa_chunks(eng):
    with eng.Fori(0, 2) as g:
        with eng.Fori(0, 2) as i:
            yield g, g * 2 + i


def pe_nsa(c, pe, cur):
    for g, ch in nsa_chunks(pe):
        pe.wait_ge(c.sem("nsa_out"), ch + 1)
        c.nc.tensor.matmul(c.PB[:, 3, :], c2(c, "rot"), c.QRAW[:, ch, :], start=True, stop=True)\
            .then_inc(c.sem("q_rot"), 1)
        pe.wait_ge(c.sem("q_ready"), ch + 1)

        def step(br, hh, qb):
            nk = nsa_nk(br, qb)
            Q = (c.QZC if br == 0 else c.QZR)[hh]
            K = (c.KC, c.KS, c.KW)[br]

            def scores(SB):
                c.nc.tensor.matmul(SB[:, :nk], Q[:, qb * P:qb * P + P], K[:, g, :nk], start=True, stop=False)
                if br == 0:
                    return c.nc.tensor.matmul(SB[:, :32], c.IDENT[:, :], c2(c, "cmask")[:, qb * 32:qb * 32 + 32],
                                              start=False, stop=True)
                return c.nc.tensor.matmul(SB[:, nk - P:nk], c.IDENT[:, :], c.CAUSAL[:, :], start=False, stop=True)

            def values(kb):
                if br == 0:
                    return c.VC[:32, g, :]
                return c.VSW[:, kb, bass.ds(g * HD + (br - 1) * P, HD)]
            return {"nk": nk, "scores": scores, "values": values,
                    "out": c.PB[:, br, qb * P + hh * HD:qb * P + hh * HD + HD]}
        pe_steps(c, pe, Steps(ch * 24 + STEPS_LAYERS, [step(*x) for x in BRANCH_STEPS], (c.PM2, c.PT2, c.SUM2)))
        pe.wait_ge(c.sem("nsa_mixed"), ch + 1)
        for qb in range(QB):
            last = c.nc.tensor.transpose(c.PB[:, 3, qb * P:qb * P + P], c.OQ2[:, qb, :], c.IDENT[:, :])
        last.then_inc(c.sem("nsa_turned"), 1)
    phase_end(c, pe, cur)


def act_nsa(c, act, cur):
    flat = c.SUM2[:, :, :].rearrange("p b e -> p (b e)")
    for g, ch in nsa_chunks(act):
        act_steps(c, act, Steps(ch * 24 + STEPS_LAYERS, [{"nk": nsa_nk(br, qb)} for br, hh, qb in BRANCH_STEPS],
                                (c.PM2, c.PT2, flat), [br * 8 + qb * 2 + hh for br, hh, qb in BRANCH_STEPS]))
        act.wait_ge(c.sem("nsa_turned"), ch + 1)
        c.nc.scalar.activation(c.YH2[:, ch + CC, :], c.PB[:, 3, :], ACT.Copy).then_inc(c.sem("nsa_hi"), 1)
    phase_end(c, act, cur)


def dve_nsa(c, dve, cur):
    V = c.nc.vector
    for Z in c.QZR + c.QZC:
        V.memset(Z[:, :], 0.0)
    dve.drain()
    for g, ch in nsa_chunks(dve):
        dve.wait_ge(c.sem("q_rot"), ch + 1)
        V.tensor_tensor(c.OB2[:, :, :].rearrange("p a b -> p (a b)"), c.PB[:, 3, :], c.SIN[:, :], ALU.mult)
        V.tensor_tensor(c.OQ2[:, :, :].rearrange("p a b -> p (a b)"), c.QRAW[:, ch, :], c.COS[:, :], ALU.mult)
        dve.drain()
        for hh in range(2):
            own = slice(hh * HD, hh * HD + HD)
            V.tensor_copy(c.QZC[hh][own, :], c.QRAW[own, ch, :])
            last = V.tensor_tensor(c.QZR[hh][own, :], c.OQ2[own, :, :].rearrange("p a b -> p (a b)"),
                                   c.OB2[own, :, :].rearrange("p a b -> p (a b)"), ALU.add)
        last.then_inc(c.sem("q_ready"), 1)
        dve_steps(c, dve, Steps(ch * 24 + STEPS_LAYERS, [{"nk": nsa_nk(br, qb)} for br, hh, qb in BRANCH_STEPS],
                                (c.PM2, c.PT2, c.SUM2)))
        V.reciprocal(c.SUM2[:, :, :], c.SUM2[:, :, :])
        dve.drain()
        for br in range(3):
            V.tensor_tensor(c.SUM2[:, br, :].rearrange("p (q h) -> p q h", h=2),
                            c.SUM2[:, br, :].rearrange("p (q h) -> p q h", h=2),
                            c.GT[:, :, bass.ds(ch * 6 + 2 * br, 2)], ALU.mult)
        dve.drain()
        V.tensor_scalar(c.SUM2[:, 0, 0:2], c.SUM2[:, 0, 0:2], c2(c, "row_ok"), None, ALU.mult)
        dve.drain()
        dve.wait_ge(c.sem("pv_done"), ch * 24 + (STEPS_LAYERS + 26))
        OQ, OB = (x[:, :, :].rearrange("p q (h d) -> p (q h) d", h=2) for x in (c.OQ2, c.OB2))
        for br in range(3):
            V.tensor_tensor(OQ if br == 0 else OB, c.PB[:, br, :].rearrange("p (e d) -> p e d", d=HD),
                            c.SUM2[:, br, :].unsqueeze(2).to_broadcast([P, 8, HD]), ALU.mult)
            dve.drain()
            if br:
                last = V.tensor_tensor(c.OQ2[:, :, :], c.OQ2[:, :, :], c.OB2[:, :, :], ALU.add)
                if br == 2:
                    last.then_inc(c.sem("nsa_mixed"), 1)
                dve.drain()
        dve.wait_ge(c.sem("nsa_hi"), ch + 1)
        V.tensor_tensor(c.YL2[:, ch + CC, :], c.PB[:, 3, :], c.YH2[:, ch + CC, :].bitcast(F32), ALU.subtract)\
            .then_inc(c.sem("nsa_out"), 1)
    phase_end(c, dve, cur)


STEPS_NSA = STEPS_LAYERS + 4 * 24


def pe_mem_kv(c, pe, cur):
    pe_normed_tile(c, pe, cur, V2 + 1, MEM)
    for tile in tiles(pe, cur, 3):
        pe_pair_tile(c, pe, tile, c.XH, c.XL, MEM)
    for tile in tiles(pe, cur, 4):
        pe_token_tile(c, pe, tile, c.XH, c.XL, MEM)
    phase_end(c, pe, cur)


def act_mem_kv(c, act, cur):
    for tile in tiles(act, cur, 4):
        act_next(c, act, tile)
        act.wait_ge(c.sem("tile_done"), tile.t + 3)
        c.nc.scalar.activation(c.MK[:, bass.ds(tile.k * 2, 2), :], c.PB[:, tile.b:tile.b + 2, :MEM], ACT.Copy)\
            .then_inc(c.sem("ps_done"), 1)
    act_values(c, act, cur, c.MV, D, MEM)
    phase_end(c, act, cur)


def dve_mem_kv(c, dve, cur):
    for _ in range(2):
        for tile in tiles(dve, cur, 4):
            dve_next(c, dve, tile)
    phase_end(c, dve, cur)


def pe_mem(c, pe, cur):
    pe_normed_tile(c, pe, cur, V2 + 2)
    for tile in tiles(pe, cur, 3):
        pe_pair_tile(c, pe, tile, c.XH, c.XL)
    phase_end(c, pe, cur)
    with pe.Fori(0, MEM_H) as h:
        pe.wait_ge(c.sem("mq_ready"), h + 1)

        def step(qb):
            def scores(SB):
                for k in range(2):
                    last = c.nc.tensor.matmul(SB[:, :MEM], c.MQS[:, k, qb * P:qb * P + P],
                                              c.MK[:, bass.ds(h * 2 + k, 1), :].rearrange("p a b -> p (a b)"),
                                              start=k == 0, stop=k == 1)
                return last
            return {"nk": MEM, "scores": scores, "values": lambda kb: c.MV[:, kb, bass.ds(h * MHD, MHD)],
                    "out": c.PB[:, qb // 2, (qb % 2) * MHD:(qb % 2) * MHD + MHD]}
        pe_steps(c, pe, Steps(h * 4 + STEPS_NSA, [step(qb) for qb in range(QB)], (c.PM3, c.PT3, c.SUM3)))
        pe.wait_ge(c.sem("mo_ready"), h + 1)
        for k in range(2):
            for qb in range(QB):
                last = c.nc.tensor.transpose(c.PB[:, 2 + k, qb * P:qb * P + P], c.OQ3[:, qb, k * P:k * P + P],
                                             c.IDENT[:, :])
        last.then_inc(c.sem("mo_turned"), 1)
    phase_end(c, pe, cur)


def act_mem(c, act, cur):
    for tile in tiles(act, cur, 4):
        act_next(c, act, tile)
        act.wait_ge(c.sem("tile_done"), tile.t + 3)
        c.nc.scalar.activation(c.MQ[:, bass.ds(tile.k * 2, 2), :], c.PB[:, tile.b:tile.b + 2, :], ACT.Copy,
                               scale=MHD ** -0.5).then_inc(c.sem("ps_done"), 1)
    phase_end(c, act, cur)
    with act.Fori(0, MEM_H) as h:
        act_steps(c, act, Steps(h * 4 + STEPS_NSA, [{"nk": MEM}] * QB, (c.PM3, c.PT3, c.SUM3), list(range(QB))))
        act.wait_ge(c.sem("mo_turned"), h + 1)
        c.nc.scalar.activation(c.YH2[:, bass.ds(h * 2, 2), :], c.PB[:, 2:4, :], ACT.Copy).then_inc(c.sem("mo_hi"), 1)
    phase_end(c, act, cur)


def dve_mem(c, dve, cur):
    V = c.nc.vector
    for tile in tiles(dve, cur, 4):
        dve_next(c, dve, tile)
    phase_end(c, dve, cur)
    with dve.Fori(0, MEM_H) as h:
        V.tensor_copy(c.MQS[:, :, :], c.MQ[:, bass.ds(h * 2, 2), :]).then_inc(c.sem("mq_ready"), 1)
        dve_steps(c, dve, Steps(h * 4 + STEPS_NSA, [{"nk": MEM}] * QB, (c.PM3, c.PT3, c.SUM3)))
        V.reciprocal(c.SUM3[:, :], c.SUM3[:, :])
        dve.drain()
        dve.wait_ge(c.sem("pv_done"), h * 4 + (STEPS_NSA + 6))
        V.tensor_tensor(c.OQ3[:, :, :], c.PB[:, 0:2, :].rearrange("p b (q d) -> p (b q) d", q=2),
                        c.SUM3[:, :].unsqueeze(2).to_broadcast([P, QB, MHD]), ALU.mult).then_inc(c.sem("mo_ready"), 1)
        dve.wait_ge(c.sem("mo_hi"), h + 1)
        V.tensor_tensor(c.YL2[:, bass.ds(h * 2, 2), :], c.PB[:, 2:4, :],
                        c.YH2[:, bass.ds(h * 2, 2), :].bitcast(F32), ALU.subtract)
        dve.drain()
    phase_end(c, dve, cur)



def pe_choose(c, pe, cur):
    for tile in tiles(pe, cur, PH):
        pe_pair_tile(c, pe, tile, c.XH, c.XL)
        pe.wait_ge(c.sem("pq_ready"), tile.k + 1)
        pe.wait_ge(c.sem("ps_scores"), tile.k + 1)
        for m in range(2):
            for tb in range(QB):
                last = c.nc.tensor.matmul(c.PB[:, 4 + m, tb * P:tb * P + P], c.QP[:, m, tb * P:tb * P + P],
                                          c.SK[:, bass.ds(tile.k * 2 + m, 1), :].rearrange("p a b -> p (a b)"),
                                          start=True, stop=True)
        last.then_inc(c.sem("key_scores"), 1)
    pe.wait_ge(c.sem("gates_chosen"), 1)
    pe.wait_ge(c.sem("picked"), PH + 2)
    for n, src in enumerate((c.RI1, c.RI2, c.RGT)):
        for tb in range(QB):
            last = c.nc.tensor.transpose(c.PB[:, n, tb * P:tb * P + P], src[:, tb, :], c.IDENT[:, :])
    last.then_inc(c.sem("turned"), 1)
    phase_end(c, pe, cur)


def act_choose(c, act, cur):
    for tile in tiles(act, cur, PH):
        act_next(c, act, tile)
        act.wait_ge(c.sem("tile_done"), tile.t + 3)
        act.wait_ge(c.sem("key_scores"), tile.k + 1)
        c.nc.scalar.activation(c.QP[:, :, :], c.PB[:, tile.b:tile.b + 2, :], ACT.Copy).then_inc(c.sem("ps_done"), 1)
        act.drain().then_inc(c.sem("pq_ready"), 1)
        act.wait_ge(c.sem("key_scores"), tile.k + 2)
        act.wait_ge(c.sem("top_done"), tile.k + 1)
        c.nc.scalar.activation(c.SC[tile.j][:, :, :, :].rearrange("p m t k -> p m (t k)"), c.PB[:, 4:6, :], ACT.Copy)\
            .then_inc(c.sem("ps_scores"), 1)
    act.wait_ge(c.sem("best_centred"), 1)
    c.nc.scalar.activation(c.RGT[:, :, :], c.RGT[:, :, :], ACT.Exp).then_inc(c.sem("best_exp"), 1)
    act.wait_ge(c.sem("turned"), 1)
    for n, dst in enumerate((c.IT1, c.IT2, c.GTT)):
        c.nc.scalar.activation(dst[:, :S], c.PB[:, n, :], ACT.Copy)
    phase_end(c, act, cur)


def dve_top16(c, dve, rows):
    V = c.nc.vector
    n = rows[0][2].shape[-1]
    left = [c.SC2[:, r * n:r * n + n] for r in range(len(rows))]
    for values, index, src in rows:
        V.max(values[:, 0:8], src)
    dve.drain()
    for (values, index, src), rest in zip(rows, left):
        V.max_index(index[:, 0:8], values[:, 0:8], src)
        V.match_replace(rest, values[:, 0:8], src, -3.0e38)
    dve.drain()
    for (values, index, src), rest in zip(rows, left):
        V.max(values[:, 8:16], rest)
    dve.drain()
    for (values, index, src), rest in zip(rows, left):
        V.max_index(index[:, 8:16], values[:, 8:16], rest)


def dve_choose(c, dve, cur):
    V = c.nc.vector
    for tile in tiles(dve, cur, PH):
        dve_next(c, dve, tile)
        s = tile.j
        dve.wait_ge(c.sem("picked"), tile.k + 1)
        dve.wait_ge(c.sem("ps_scores"), tile.k + 2)
        carry_wait(c, dve)
        dve_top16(c, dve, [(c.TV[:, m, tb, :], c.TI[:, m, tb, :], c.SC[s][:, m, tb, :])
                           for m in range(2) for tb in range(QB)])
        dve.drain().then_inc(c.sem("top_done"), 1)
        V.tensor_copy(c.TF[s][:, :, :, :], c.TI[:, :, :, :])
        V.tensor_tensor(c.CAND[:, :, :].rearrange("p t (a b) -> p t a b", a=TOPK),
                        c.TV[:, 0, :, :].unsqueeze(3).to_broadcast([P, QB, TOPK, TOPK]),
                        c.TV[:, 1, :, :].unsqueeze(2).to_broadcast([P, QB, TOPK, TOPK]), ALU.add)
        dve.drain()
        dve_top16(c, dve, [(c.BV[:, tb, :], c.BI[:, 0, tb, :], c.CAND[:, tb, :]) for tb in range(QB)])
        dve.drain()
        V.tensor_copy(c.GS[:, 0, 0:QB], c.BV[:, :, 0])
        V.tensor_scalar(c.BI[:, 1], c.BI[:, 0], 4, None, ALU.logical_shift_right)
        V.tensor_scalar(c.BI[:, 2], c.BI[:, 0], 15, None, ALU.bitwise_and)
        dve.drain()
        V.tensor_tensor(c.RGT[:, :, bass.ds(tile.k * TOPK, TOPK)], c.BV[:, :, :],
                        c.GS[:, 0, 0:QB].unsqueeze(2).to_broadcast([P, QB, TOPK]), ALU.subtract)
        V.tensor_copy(c.BF[s][:, :, :, :], c.BI[:, 1:3]).then_inc(c.sem("places"), 1)
        dve.drain()
    dve.drain().then_inc(c.sem("best_centred"), 1)
    E = c.SC2[:, :].rearrange("p (t a b) -> p t a b", t=QB, a=TOPK)
    V.tensor_tensor(E, c.BF[1][:, 1].unsqueeze(3).to_broadcast([P, QB, TOPK, TOPK]),
                    c2(c, "iota")[:, 0:TOPK].unsqueeze(1).unsqueeze(1).to_broadcast([P, QB, TOPK, TOPK]), ALU.is_equal)
    dve.drain()
    V.tensor_tensor(E, E, c.TF[1][:, 1].unsqueeze(2).to_broadcast([P, QB, TOPK, TOPK]), ALU.mult)
    dve.drain()
    V.reduce_sum(c.RI2[:, :, (PH - 1) * TOPK:], E, axis=AX.X)
    dve.wait_ge(c.sem("best_exp"), 1)
    G = c.RGT[:, :, :].rearrange("p t (h k) -> p (t h) k", h=PH)
    V.reduce_sum(c.GS[:, 1, :], G, axis=AX.X)
    dve.drain()
    V.reciprocal(c.GS[:, 1, :], c.GS[:, 1, :])
    dve.drain()
    V.tensor_tensor(G, G, c.GS[:, 1, :].unsqueeze(2).to_broadcast([P, QB * PH, TOPK]), ALU.mult)
    dve.drain().then_inc(c.sem("gates_chosen"), 1)
    V.memset(c.IT2[:, S:], 0.0)
    phase_end(c, dve, cur)


def pool_choose(c, pool):
    G = c.nc.gpsimd
    iota16 = c2(c, "iota")[:, 0:TOPK]

    def pick(i, s, sets):
        for m, R in enumerate((c.RI1, c.RI2)[:sets]):
            G.tensor_tensor(c.EQ[:, :, :, :], c.BF[s][:, m].unsqueeze(3).to_broadcast([P, QB, TOPK, TOPK]),
                            iota16.unsqueeze(1).unsqueeze(1).to_broadcast([P, QB, TOPK, TOPK]), ALU.subtract)
            pool.drain()
            G.tensor_scalar(c.EQ[:, :, :, :], c.EQ[:, :, :, :], 0.0, None, ALU.is_equal)
            pool.drain()
            G.tensor_tensor(c.EQ[:, :, :, :], c.EQ[:, :, :, :],
                            c.TF[s][:, m].unsqueeze(2).to_broadcast([P, QB, TOPK, TOPK]), ALU.mult)
            for w in (8, 4, 2, 1):
                pool.drain()
                out = c.EQ[:, :, :, 0:w] if w > 1 else R[:, :, bass.ds(i * 2 * TOPK + s * TOPK, TOPK)].unsqueeze(3)
                G.tensor_tensor(out, c.EQ[:, :, :, 0:w], c.EQ[:, :, :, w:2 * w], ALU.add)
            pool.drain()
        pool.drain().then_inc(c.sem("picked"), 1)
    with pool.Fori(0, PH // 2 - 1) as i:
        for s in range(2):
            pool.wait_ge(c.sem("places"), i * 2 + (s + 1))
            carry_wait(c, pool)
            pick(i, s, 2)
    for s in range(2):
        pool.wait_ge(c.sem("places"), PH - 1 + s)
        pick(PH // 2 - 1, s, 2 - s)


GROUPS = S // 4
BLOCKS = S // TOK_BLOCK
PER_BLOCK = TOK_BLOCK // 4


def pe_gates(c, pe, cur):
    with pe.Fori(0, GROUPS // 2) as i:
        for j in range(2):
            pe.wait_ge(c.sem("hot_dve"), i * 2 + (j + 1))
            pe.wait_ge(c.sem("hot_act"), i * 2 + (j + 1))
            pe.wait_ge(c.sem("hot_pool"), i * 2 + (j + 1))
            pe.wait_ge(c.sem("gm_copied"), i * 2 + (j + 1))
            for q in range(4):
                last = c.nc.tensor.matmul(c.PB[:, j, q * P:q * P + P], c.OA[j][:, q, :], c.OB[j][:, q, :],
                                          start=True, stop=True)
            last.then_inc(c.sem("gm_full"), 1)
    phase_end(c, pe, cur)


def act_gates(c, act, cur, gm):
    A = c.nc.scalar

    def hot(j, group):
        A.activation(c.HS[j][:, :], c2(c, "iota"), ACT.Square, scale=-1.0, bias=c.IT2[:, bass.ds(group * 4, 1)])
        act.drain()
        A.activation(c.OB[j][:, 0, :], c.HS[j][:, :], ACT.Relu, scale=-1.0, bias=c.ONES[:, 0:1])\
            .then_inc(c.sem("hot_act"), 1)
    hot(0, 0)
    hot(1, 1)
    with act.Fori(0, BLOCKS // 2) as i:
        for s in range(2):
            act.wait_ge(c.sem(f"gm_stored{s}"), i * 16 + 16)
            for q in range(PER_BLOCK):
                act.wait_ge(c.sem("gm_full"), (i * 2 + s) * PER_BLOCK + (q + 3))
                hot(q % 2, (i * 2 + s) * PER_BLOCK + (q + 2))
                c.nc.scalar.activation(c.STG[s][:, :, q * 4:q * 4 + 4].rearrange("p e t -> p t e"),
                                       c.PB[:, q % 2, :].rearrange("p (t e) -> p t e", t=4), ACT.Copy)\
                    .then_inc(c.sem("gm_copied"), 1)
            act.drain()
            act.dma_start(gm[bass.ds(i * 2 + s, 1)].rearrange("b p e t -> (b p) e t"), c.STG[s][:, :, :])\
                .then_inc(c.sem(f"gm_stored{s}"), 16)
    phase_end(c, act, cur)


def dve_gates(c, dve, cur):
    V = c.nc.vector
    iota = c2(c, "iota")
    with dve.Fori(0, GROUPS // 2) as i:
        for j in range(2):
            dve.wait_ge(c.sem("gm_full"), i * 2 + (j + 1))
            for q in range(4):
                tok = i * 8 + (4 * j + q)
                last = V.tensor_scalar(c.OA[j][:, q, :], iota, c.IT1[:, bass.ds(tok, 1)],
                                       c.GTT[:, bass.ds(tok, 1)], ALU.is_equal, ALU.mult)
                if q in (1, 2):
                    V.tensor_scalar(c.OB[j][:, q, :], iota, c.IT2[:, bass.ds(tok, 1)], None, ALU.is_equal)
            last.then_inc(c.sem("hot_dve"), 1)
    phase_end(c, dve, cur)


def pool_gates(c, pool):
    G = c.nc.gpsimd
    with pool.Fori(0, GROUPS // 2) as i:
        for j in range(2):
            pool.wait_ge(c.sem("gm_full"), i * 2 + (j + 1))
            carry_wait(c, pool)
            G.tensor_tensor(c.HP[j][:, :], c2(c, "iota"), c.IT2[:, bass.ds(i * 8 + (4 * j + 3), 1)].to_broadcast([P, P]),
                            ALU.subtract)
            pool.drain()
            G.tensor_scalar(c.OB[j][:, 3, :], c.HP[j][:, :], 0.0, None, ALU.is_equal).then_inc(c.sem("hot_pool"), 1)



def expert_blocks(eng, body):
    body(0, 0, True, False)
    with eng.Fori(0, (N_EXP - 2) // 2) as i:
        for j in (1, 2):
            body(i * 2 + j, j % 2, False, False)
    body(N_EXP - 1, (N_EXP - 1) % 2, False, True)


def pe_experts(c, pe, cur):
    T = c.nc.tensor

    def act_in(e, s):
        p = (T_PEER + s) % 2
        W = [x[p][:, :D].rearrange("p (k c) -> p k c", k=DC) for x in (c.WH, c.WL)]
        for k in range(DC):
            last = mm3(c, c.PB[:, s, :], W[0][:, k, :], W[1][:, k, :], c.XH[:, k, :], c.XL[:, k, :],
                       k == 0, k == DC - 1)
        last.then_inc(c.sem("a_done"), 1)

    def body(e, s, first, final):
        if first:
            pe.wait_ge(c.sem("w_split"), T_PEER + 1)
            act_in(e, s)
        if not final:
            pe.wait_ge(c.sem("u_split"), e + 1)
            if not first:
                pe.wait_ge(c.sem("gelu"), e)
            act_in(e + 1, 1 - s)
        pe.wait_ge(c.sem("w_split"), e + (T_PEER + 1))
        pe.wait_ge(c.sem("wg_split"), e + 1)
        p = (T_PEER + s) % 2
        W = [x[p][:, D:] for x in (c.WH, c.WL)]
        for r in range(4):
            m = 4 + r
            pe.wait_ge(c.sem("y_added"), e * 4 + (r + 1))
            mm3(c, c.PB[:, 2 + r % 2, :], W[0][:, m * P:m * P + P], W[1][:, m * P:m * P + P],
                c.WGH[:, s, :], c.WGL[:, s, :], True, True).then_inc(c.sem("y_part"), 1)
            last = mm3(c, c.PB[:, 4 + r, :], W[0][:, r * P:r * P + P], W[1][:, r * P:r * P + P],
                       c.WGH[:, s, :], c.WGL[:, s, :], first, final)
        last.then_inc(c.sem("y_done"), 1)
    expert_blocks(pe, body)


def act_experts(c, act, cur):
    A = c.nc.scalar

    def body(e, s, first, final):
        p = (T_PEER + 1 + s) % 2
        if not final:
            act.wait_ge(c.sem(f"w_loaded{p}"), (e + (T_PEER + 1 - p)) * 8 + 16)
            if not first:
                act.wait_ge(c.sem("a_done"), e)
            A.activation(c.WH[p][:, :D], c.RAW[p][:, :D], ACT.Copy).then_inc(c.sem("u_hi"), 1)
        act.wait_ge(c.sem("a_done"), e + 1)
        A.activation(c.AG[:, s, :], c.PB[:, s, :], ACT.Gelu_apprx_tanh).then_inc(c.sem("gelu"), 1)
        act.wait_ge(c.sem("wg_ready"), e + 1)
        if not first:
            act.wait_ge(c.sem("y_done"), e)
        A.activation(c.WGH[:, s, :], c.WG[:, s, :], ACT.Copy).then_inc(c.sem("wg_hi"), 1)
        if not final:
            if not first:
                act.wait_ge(c.sem("y_done"), e + 1)
            A.activation(c.WH[p][:, D:], c.RAW[p][:, D:], ACT.Copy).then_inc(c.sem("v_hi"), 1)
    expert_blocks(act, body)


def dve_experts(c, dve, cur):
    V = c.nc.vector

    def add(e_before, r):
        dve.wait_ge(c.sem("y_part"), e_before * 4 + (r + 1))
        V.tensor_tensor(c.YACC[:, r, :], c.YACC[:, r, :], c.PB[:, 2 + r % 2, :], ALU.add)\
            .then_inc(c.sem("y_added"), 1)

    def body(e, s, first, final):
        p = (T_PEER + 1 + s) % 2
        if not final:
            dve.wait_ge(c.sem("u_hi"), e + 1)
            V.tensor_tensor(c.WL[p][:, :D], c.RAW[p][:, :D], c.WH[p][:, :D].bitcast(F32), ALU.subtract)\
                .then_inc(c.sem("u_split"), 1)
        dve.wait_ge(c.sem("gelu"), e + 1)
        dve.wait_ge(c.sem(f"gm_loaded{s}"), (e - s) * 8 + 16)
        if first:
            V.memset(c.YACC[:, :, :], 0.0)
        V.tensor_tensor(c.WG[:, s, :], c.AG[:, s, :], c.GM[s][:, :], ALU.mult).then_inc(c.sem("wg_ready"), 1)
        if not first:
            add(e - 1, 0)
            add(e - 1, 1)
        dve.wait_ge(c.sem("wg_hi"), e + 1)
        V.tensor_tensor(c.WGL[:, s, :], c.WG[:, s, :], c.WGH[:, s, :].bitcast(F32), ALU.subtract)\
            .then_inc(c.sem("wg_split"), 1)
        if not first:
            add(e - 1, 2)
            add(e - 1, 3)
        if not final:
            dve.wait_ge(c.sem("v_hi"), e + 1)
            V.tensor_tensor(c.WL[p][:, D:], c.RAW[p][:, D:], c.WH[p][:, D:].bitcast(F32), ALU.subtract)\
                .then_inc(c.sem("w_split"), 1)
    expert_blocks(dve, body)
    for r in range(4):
        add(N_EXP - 1, r)
    dve.drain()
    dve.wait_ge(c.sem("y_done"), N_EXP + 1)
    for m in (0, 2):
        V.tensor_tensor(c.X[:, m:m + 2, :], c.X[:, m:m + 2, :], c.PB[:, 4 + m:6 + m, :], ALU.add)\
            .then_inc(c.sem("x_new"), 1)
    for m in (0, 2):
        V.tensor_tensor(c.X[:, 4 + m:6 + m, :], c.X[:, 4 + m:6 + m, :], c.YACC[:, m:m + 2, :], ALU.add)\
            .then_inc(c.sem("x_new"), 1)


def pool_gate_loads(c, pool, gm):
    def load(e, s, wait):
        if wait:
            pool.wait_ge(c.sem("wg_ready"), e - 1)
        pool.dma_start(c.GM[s][:, :].rearrange("p (b t) -> p b t", b=BLOCKS),
                       gm[:, :, bass.ds(e, 1), :].rearrange("b p e t -> p b (e t)")).then_inc(c.sem(f"gm_loaded{s}"), 16)
    for s in range(2):
        pool.wait_ge(c.sem(f"gm_stored{s}"), BLOCKS // 2 * 16 + 16)
    load(0, 0, False)
    load(1, 1, False)
    with pool.Fori(1, N_EXP // 2) as i:
        for s in range(2):
            load(i * 2 + s, s, True)


V2 = 3 * LAYERS
PH2 = LAYERS * PHASES_LAYER


def pe_second(c, pe, cur):
    def norm(v, width=S, bank=4):
        pe_norm(c, pe, V2 + v, width, bank)
    norm(0, bank=0)
    pe_proj2(c, pe, cur)
    pe_nsa(c, pe, cur)
    pe_residual(c, pe, cur, c.YH2, c.YL2)
    norm(1, MEM)
    pe_mem_kv(c, pe, cur)
    norm(2)
    pe_mem(c, pe, cur)
    pe_residual(c, pe, cur, c.YH2, c.YL2)
    norm(3)
    pe.wait_ge(c.sem("xn_lo"), (V2 + 4) * DC)
    pe.wait_ge(c.sem("sk_loaded"), 16)
    pe_choose(c, pe, cur)
    pe_gates(c, pe, cur)
    pe_experts(c, pe, cur)
    pe_norm(c, pe, V2 + 4, bank=0)


def act_second(c, act, cur, gm):
    def norm(v, X=None, width=S, bank=4, news=None):
        act_norm(c, act, V2 + v, c.X if X is None else X, c.XH, width, bank, news)
    norm(0, bank=0, news=V2 * 4)
    act_proj2(c, act, cur)
    act_nsa(c, act, cur)
    act_residual(c, act, cur)
    act.wait_ge(c.sem("mem_loaded"), 16)
    norm(1, c.MEMX, MEM)
    act_mem_kv(c, act, cur)
    norm(2)
    act_mem(c, act, cur)
    act_residual(c, act, cur)
    norm(3)
    act_choose(c, act, cur)
    act_gates(c, act, cur, gm)
    act_experts(c, act, cur)
    act_norm(c, act, V2 + 4, c.X, None, bank=0, news=V2 * 4 + 4)


def dve_second(c, dve, cur):
    def norm(v, g, X=None, width=S):
        dve_norm(c, dve, V2 + v, c.X if X is None else X, lambda k: p2(c, g, k, 1), c.XH, c.XL, width)
    norm(0, "mix_g")
    dve_proj2(c, dve, cur)
    dve_nsa(c, dve, cur)
    dve_residual(c, dve, cur)
    dve.wait_ge(c.sem("mem_loaded"), 16)
    norm(1, "memkv_g", c.MEMX, MEM)
    dve_mem_kv(c, dve, cur)
    norm(2, "memq_g")
    dve_mem(c, dve, cur)
    dve_residual(c, dve, cur)
    norm(3, "peer_g")
    dve_choose(c, dve, cur)
    dve_gates(c, dve, cur)
    dve_experts(c, dve, cur)
    dve_norm(c, dve, V2 + 4, c.X, lambda k: p2(c, "final_g", k, 1), None, None, out=c.FIN)


def pool_second(c, pool, d):
    pool.wait_ge(c.sem("xn_ready"), V2 * DC + 1)
    pool.dma_start(c.SGB[:, 0, :].bitcast(I32), d["positions"]).then_inc(c.sem("pos_loaded"), 16)
    pool.wait_ge(c.sem("phase_done"), (PH2 + 3) * 3)
    pool.dma_start(c.MEMX[:, :, :], d["mem"]).then_inc(c.sem("mem_loaded"), 16)
    pool.wait_ge(c.sem("phase_done"), (PH2 + 7) * 3)
    pool.wait_ge(c.sem("xn_ready"), (V2 + 3) * DC + 1)
    pool.dma_start(c.SK[:, :, :], d["sub_keys"]).then_inc(c.sem("sk_loaded"), 16)
    pool_choose(c, pool)
    pool.wait_ge(c.sem("phase_done"), (PH2 + 8) * 3)
    pool_gates(c, pool)
    pool.wait_ge(c.sem("phase_done"), (PH2 + 9) * 3)
    pool_gate_loads(c, pool, d["gate_matrix"])


def build(nc, d, out):
    with ExitStack() as stack:
        c = Ctx(nc, stack)
        allocate(c)
        block = stack.enter_context(nc.Block())

        @block.sync
        def _(sp):
            sp_setup(c, sp, d)
            sp_weight_loads(c, sp, lambda t: d["weights"][t], 0, NT)
            for k in range(DC):
                sp.wait_ge(c.sem("xn_ready"), (V2 + 4) * DC + k + 1)
                sp.dma_start(out[:, k, :], c.FIN[:, k, :]).then_inc(c.sem("out_stored"), 16)
            sp.wait_ge(c.sem("out_stored"), 16 * DC)

        @block.gpsimd
        def _(pool):
            pool_second(c, pool, d)

        @block.tensor
        def _(pe):
            pe_setup(c, pe)
            cur = Cursor()
            with pe.Fori(0, LAYERS) as l:
                cur.enter_layer(l)
                pe_layer(c, pe, cur, l)
            cur.leave_layers()
            pe_second(c, pe, cur)

        @block.scalar
        def _(act):
            act_setup(c, act)
            act_split(c, act, 0, 0, 0)
            cur = Cursor()
            with act.Fori(0, LAYERS) as l:
                cur.enter_layer(l)
                act_layer(c, act, cur, l)
            cur.leave_layers()
            act_second(c, act, cur, d["gate_matrix"])

        @block.vector
        def _(dve):
            dve_setup(c, dve)
            dve_split(c, dve, 0, 0)
            cur = Cursor()
            with dve.Fori(0, LAYERS) as l:
                cur.enter_layer(l)
                dve_layer(c, dve, cur, l)
            cur.leave_layers()
            dve_second(c, dve, cur)



def by_chunks(w, chunks):
    k = w.shape[0] // P
    return np.stack([w[:, a:a + P].reshape(k, P, P) for a in chunks], 2).transpose(1, 0, 2, 3).reshape(P, -1)


def by_columns(w, at, n=256):
    return w[:, at:at + n].reshape(w.shape[0] // P, P, n).transpose(1, 0, 2).reshape(P, -1)


def padded(t):
    out = np.zeros((P, TILE), t.dtype)
    out[:, :t.shape[1]] = t
    return out


OFF_LX, OFF_LG, OFF_Q, OFF_K, OFF_V, OFF_F, OFF_GATE = 0, 1024, 2048, 3072, 4096, 5120, 5136


def layer_tiles(a, l):
    w_in = a["w_in"][l]

    def ffn(n):
        up, down = a[f"w_up{n}"][l], a[f"w_down{n}"][l]
        return ([by_chunks(up, (j * P, F_FF + j * P)) for j in range(FC)]
                + [down[i * 256:i * 256 + 256].reshape(2, P, D).transpose(1, 0, 2).reshape(P, -1)
                   for i in range(FC // 2)])

    def gated(branch, w):
        out = []
        for half in (0, 2):
            for j in (half, half + 1):
                g = OFF_GATE + branch * D + j * 256
                out.append(by_chunks(w_in, (g, g + P)))
            for j in (half, half + 1):
                out.append(by_chunks(w, (j * 256, j * 256 + P)))
        return out
    f = w_in[:, OFF_F:OFF_F + HEADS]
    f4 = np.zeros((D, P), f.dtype)
    for r in (0, 32, 64, 96):
        f4[:, r:r + HEADS] = f
    wax = np.stack([a["w_a"][l], a["w_x"][l]]).transpose(2, 0, 1, 3).reshape(P, -1)
    out = ffn(1)
    out += [by_chunks(w_in, (OFF_LX + j * 256, OFF_LX + j * 256 + P)) for j in range(4)]
    gelu = [by_chunks(w_in, (OFF_LG + j * 256, OFF_LG + j * 256 + P)) for j in range(4)]
    out += [gelu[0], wax] + gelu[1:] + gated(0, a["w_lru_out"][l])
    out += [padded(by_columns(f4, 0, P))]
    out += [by_columns(w_in, OFF_V + j * 256) for j in range(4)]
    out += [by_chunks(w_in, (OFF_Q + i * P, OFF_K + i * P)) for i in range(HEADS // 2)]
    out += gated(1, a["w_attn_out"][l])
    out += [by_chunks(a["w_o"][l], (j * 256, j * 256 + P)) for j in range(4)]
    out += ffn(2)
    assert len(out) == TL
    return out


def chunked(v):
    return v.reshape(-1, P).T


def layer_params(a, l):
    f4 = np.zeros((P, 1), np.float32)
    for r in (0, 32, 64, 96):
        f4[r:r + HEADS, 0] = a["b_forget"][l]
    cols = {"g_ffn1": chunked(a["g_ffn1"][l]), "g_mix": chunked(a["g_mix"][l]), "g_ffn2": chunked(a["g_ffn2"][l]),
            "b_gate": chunked(a["b_gate"][l]),
            "conv_w": a["conv_w"][l].reshape(4, DC, P).transpose(2, 1, 0).reshape(P, -1),
            "conv_b": chunked(a["conv_b"][l]), "b_a": chunked(a["b_a"][l]), "b_x": chunked(a["b_x"][l]),
            "lam": chunked(a["lam"][l]), "b_f": f4,
            "g_q": np.concatenate([a["g_q"][l]] * 2)[:, None], "g_k": np.concatenate([a["g_k"][l]] * 2)[:, None]}
    return np.concatenate([cols[n] for n in PRM], 1)


def second_tiles(a):
    w = a["w_in_2"][0]
    A, B, Q, KC_, VC_, KS_, VS_, KW_, VW_, G = np.cumsum([0, 512, 512, 512, 128, 128, 128, 128, 128, 128])

    def doubled(at):
        g = w[:, at:at + P].reshape(D, 2, 1, HD)
        return by_chunks(np.concatenate([g, g], 2).reshape(D, 256), (0, P))
    out = [by_chunks(w, (A + j * P, B + j * P)) for j in range(4)]
    out += [by_chunks(w, (Q + j * 256, Q + j * 256 + P)) for j in range(2)]
    out += [by_chunks(w, (KC_, VC_)), doubled(KS_), doubled(KW_)]
    out += [by_columns(np.concatenate([w[:, VS_:VS_ + P], w[:, VW_:VW_ + P]], 1), 0)]
    gates = w[:, G:G + 24].reshape(D, 4, 2, 3).transpose(0, 1, 3, 2).reshape(D, 24)
    out += [padded(by_columns(gates, 0, 24))]
    for kv in range(2):
        w1 = a["cmp_w1_2"][0, kv].reshape(32, HD, P).transpose(1, 0, 2)
        w1 = np.concatenate([w1, w1], 0)
        out += [w1[:, h * 16:h * 16 + 16].reshape(P, -1) for h in range(2)]
    pairs = [(j * 256, j * 256 + P) for j in range(4)]
    out += [by_chunks(a["w_out_2"][0], x) for x in pairs]
    out += [by_chunks(a["w_mem_k_2"][0], x) for x in pairs]
    out += [by_columns(a["w_mem_v_2"][0], j * 256) for j in range(4)]
    out += [by_chunks(a["w_mem_q_2"][0], x) for x in pairs]
    out += [by_chunks(a["w_mem_o_2"][0], x) for x in pairs]
    out += [by_chunks(a["peer_w_q_2"][0], (h * 256, h * 256 + P)) for h in range(PH)]
    return out


def expert_tiles(a):
    u = a["peer_u_2"][0].reshape(KEYS, KEYS, DC, P)
    v = a["peer_v_2"][0].reshape(KEYS, KEYS, D)
    return np.concatenate([u.transpose(1, 3, 2, 0).reshape(KEYS, P, D), v.transpose(1, 0, 2)], 2)


def second_params(a):
    two = lambda v: np.concatenate([v, v], 0)
    cols = {"mix_g": chunked(a["mix_norm_g_2"][0]),
            "dw_w": a["conv_dw_w_2"][0].reshape(CONV_K, CC, P).transpose(2, 1, 0).reshape(P, -1),
            "dw_b": chunked(a["conv_dw_b_2"][0]), "ln_g": chunked(a["conv_ln_g_2"][0]),
            "ln_b": chunked(a["conv_ln_b_2"][0]), "cmp_b1": a["cmp_b1_2"][0].T,
            "cmp_b2k": two(a["cmp_b2_2"][0, 0])[:, None],
            "cmp_b2v": np.stack([a["cmp_b2_2"][0, 1]] * P),
            "cmp_pos": two(a["cmp_pos_2"][0].transpose(2, 0, 1).reshape(HD, 64)),
            "cmp_w2k": np.concatenate([a["cmp_w2_2"][0, 0]] * 2, 1), "cmp_w2v": a["cmp_w2_2"][0, 1],
            "memq_g": chunked(a["mem_q_norm_g_2"][0]), "memkv_g": chunked(a["mem_kv_norm_g_2"][0]),
            "peer_g": chunked(a["peer_norm_g_2"][0]), "final_g": chunked(a["final_norm_g_2"])}
    return np.concatenate([cols[n] for n in PRM2], 1)


def features_first(x):
    return np.ascontiguousarray(x.T.reshape(DC, P, -1).transpose(1, 0, 2))


def kernel(**inputs):
    import concourse.bacc as bacc
    from concourse.bass_utils import run_bass_kernel_spmd

    a = {n: np.asarray(v) for n, v in inputs.items()}
    tiles_ = layer_tiles(a, 0) + layer_tiles(a, 1) + second_tiles(a)
    arrays = {
        "x": features_first(a["x"][0]),
        "weights": np.concatenate([np.stack(tiles_), expert_tiles(a)], 0),
        "params": np.ascontiguousarray(np.stack([layer_params(a, l) for l in range(LAYERS)], 1)),
        "params2": np.ascontiguousarray(second_params(a)),
        "consts": constants(), "consts2": constants2(),
        "positions": np.stack([a["positions_2"][0]] * P),
        "mem": features_first(a["mem_2"][0]),
        "sub_keys": np.ascontiguousarray(a["peer_sub_keys_2"][0].transpose(3, 0, 1, 2).reshape(P, 2 * PH, KEYS)),
    }
    nc = bacc.Bacc("TRN2", target_bir_lowering=False, num_devices=1)
    d = {n: nc.dram_tensor(n, v.shape, mybir.dt.from_np(v.dtype), kind="ExternalInput").ap()
         for n, v in arrays.items()}
    d["gate_matrix"] = nc.dram_tensor("gate_matrix", (BLOCKS, P, KEYS, TOK_BLOCK), F32, kind="Internal").ap()
    out = nc.dram_tensor("out", (P, DC, S), F32, kind="ExternalOutput").ap()
    build(nc, d, out)
    r = run_bass_kernel_spmd(nc, [arrays], core_ids=[0]).results[0]["out"]
    return r.transpose(1, 0, 2).reshape(D, S).T.reshape(1, S, D)
```
